# Optimizing a Trainium2 kernel written in Bass

```python
import jax, jax.numpy as jnp
from jax import lax
import numpy as np
import jax
import jax.numpy as jnp

D_MODEL = 1024
BATCH = 1
SEQ = 512
DEPTH = 2

N_MIXERS = 2
N_LAYERS_A = (DEPTH + N_MIXERS - 1) // N_MIXERS
N_LAYERS_B = DEPTH // N_MIXERS
LRU_WIDTH = D_MODEL
LRU_HEADS = 4
LRU_HEAD_DIM = LRU_WIDTH // LRU_HEADS
CONV_WIDTH = 4
LRU_C = 8.0
MIN_RAD = 0.9
MAX_RAD = 0.999
POOL_WINDOWS = (2, 4, 8, 16)
POOL_GROUPS = len(POOL_WINDOWS)
POOL_GROUP_DIM = D_MODEL // POOL_GROUPS
D_FF = 4 * D_MODEL
N_MOD = 6
EPS = 1e-6


def rms_norm(x, g):
    xf = x.astype(jnp.float32)
    y = xf * lax.rsqrt(jnp.mean(xf * xf, axis=-1, keepdims=True) + EPS)
    return (y * g.astype(jnp.float32)).astype(x.dtype)

def modulate(h, shift, scale):
    return h * (1.0 + scale[:, None, :]) + shift[:, None, :]

def causal_depthwise_conv(x, w, b):
    s = x.shape[1]
    xp = jnp.pad(x, ((0, 0), (CONV_WIDTH - 1, 0), (0, 0)))
    y = xp[:, 0:s] * w[0]
    for k in range(1, CONV_WIDTH):
        y = y + xp[:, k:k + s] * w[k]
    return y + b

def _lru_combine(left, right):
    a1, b1 = left
    a2, b2 = right
    return a1 * a2, a2 * b1 + b2

def block_diag_linear(x, w, b):
    bsz, s, _ = x.shape
    xh = x.reshape(bsz, s, LRU_HEADS, LRU_HEAD_DIM)
    y = jnp.einsum("bshi,hij->bshj", xh, w) + b
    return y.reshape(bsz, s, LRU_WIDTH)

def rg_lru(x, w_a, b_a, w_x, b_x, lam):
    gate_r = jax.nn.sigmoid(block_diag_linear(x, w_a, b_a)).astype(jnp.float32)
    gate_i = jax.nn.sigmoid(block_diag_linear(x, w_x, b_x)).astype(jnp.float32)
    log_a = LRU_C * gate_r * jax.nn.log_sigmoid(lam.astype(jnp.float32))
    a = jnp.exp(log_a)
    mult = jnp.sqrt(-jnp.expm1(2.0 * log_a))
    u = mult * (gate_i * x.astype(jnp.float32))
    _, h = lax.associative_scan(_lru_combine, (a, u), axis=1)
    return h.astype(x.dtype)

def recurrent_mixer(h, w_y, b_y, w_in, b_in, conv_w, conv_b, w_a, b_a, w_x, b_x, lam, w_out, b_out):
    gate_branch = jax.nn.gelu(jnp.einsum("bsd,dw->bsw", h, w_y) + b_y)
    xr = jnp.einsum("bsd,dw->bsw", h, w_in) + b_in
    xr = causal_depthwise_conv(xr, conv_w, conv_b)
    xr = rg_lru(xr, w_a, b_a, w_x, b_x, lam)
    return jnp.einsum("bsw,wd->bsd", xr * gate_branch, w_out) + b_out

def pool_mixer(h, w_pool, pool_scale):
    bsz, s, _ = h.shape
    hf = h.astype(jnp.float32)
    counts = jnp.arange(1, s + 1, dtype=jnp.float32)
    outs = []
    for g, win in enumerate(POOL_WINDOWS):
        xg = hf[..., g * POOL_GROUP_DIM:(g + 1) * POOL_GROUP_DIM]
        cs = jnp.cumsum(xg, axis=1)
        cs_lag = jnp.pad(cs, ((0, 0), (win, 0), (0, 0)))[:, :s]
        mean = (cs - cs_lag) / jnp.minimum(counts, float(win))[None, :, None]
        outs.append(mean - xg)
    pooled = jnp.stack(outs, axis=2).astype(h.dtype)
    mixed = jnp.einsum("bsgi,gij->bsgj", pooled, w_pool).reshape(bsz, s, D_MODEL)
    return mixed * pool_scale

def sq_relu_mlp(h, w1, w2):
    u = jax.nn.relu(jnp.einsum("bsd,df->bsf", h, w1))
    return jnp.einsum("bsf,fd->bsd", u * u, w2)

def first_inputs(seed: int = 0) -> dict:
    key = jax.random.key(seed)
    ks = jax.random.split(key, 26)
    f32 = jnp.float32
    nrm = lambda k, shape, s: (jax.random.normal(k, shape, f32) * s)
    d, w, hd, na, nb = D_MODEL, LRU_WIDTH, LRU_HEAD_DIM, N_LAYERS_A, N_LAYERS_B
    rad = jnp.sqrt(jax.random.uniform(ks[15], (na, w), f32, MIN_RAD ** 2, MAX_RAD ** 2))
    return {
        "x": nrm(ks[0], (BATCH, SEQ, d), 1.0),
        "c": nrm(ks[1], (BATCH, d), 1.0),
        "w_mod": nrm(ks[2], (DEPTH, d, N_MOD * d), 0.5 * d ** -0.5),
        "b_mod": nrm(ks[3], (DEPTH, N_MOD * d), 0.02),
        "norm_mix_g": 1.0 + nrm(ks[4], (DEPTH, d), 0.05),
        "norm_ffn_g": 1.0 + nrm(ks[5], (DEPTH, d), 0.05),
        "lru_w_y": nrm(ks[6], (na, d, w), d ** -0.5),
        "lru_b_y": nrm(ks[7], (na, w), 0.02),
        "lru_w_in": nrm(ks[8], (na, d, w), d ** -0.5),
        "lru_b_in": nrm(ks[9], (na, w), 0.02),
        "lru_conv_w": nrm(ks[10], (na, CONV_WIDTH, w), CONV_WIDTH ** -0.5),
        "lru_conv_b": nrm(ks[11], (na, w), 0.02),
        "lru_w_a": nrm(ks[12], (na, LRU_HEADS, hd, hd), hd ** -0.5),
        "lru_b_a": nrm(ks[13], (na, LRU_HEADS, hd), 0.02),
        "lru_w_x": nrm(ks[14], (na, LRU_HEADS, hd, hd), hd ** -0.5),
        "lru_b_x": nrm(ks[16], (na, LRU_HEADS, hd), 0.02),
        "lru_lambda": jnp.log(rad) - jnp.log1p(-rad),
        "lru_w_out": nrm(ks[17], (na, w, d), w ** -0.5),
        "lru_b_out": nrm(ks[18], (na, d), 0.02),
        "pool_w": nrm(ks[19], (nb, POOL_GROUPS, POOL_GROUP_DIM, POOL_GROUP_DIM), POOL_GROUP_DIM ** -0.5),
        "pool_scale": 1.0 + nrm(ks[20], (nb, d), 0.1),
        "ffn_w1": nrm(ks[21], (DEPTH, d, D_FF), d ** -0.5),
        "ffn_w2": nrm(ks[22], (DEPTH, D_FF, d), D_FF ** -0.5),
        "final_norm_g": 1.0 + nrm(ks[23], (d,), 0.05),
    }

def first_block(x, c, w_mod, b_mod, norm_mix_g, norm_ffn_g, lru_w_y, lru_b_y, lru_w_in, lru_b_in,
              lru_conv_w, lru_conv_b, lru_w_a, lru_b_a, lru_w_x, lru_b_x, lru_lambda, lru_w_out,
              lru_b_out, pool_w, pool_scale, ffn_w1, ffn_w2, final_norm_g):
    cond = jax.nn.silu(c)
    for i in range(DEPTH):
        mod = jnp.einsum("bd,de->be", cond, w_mod[i]) + b_mod[i]
        sh_m, sc_m, gt_m, sh_f, sc_f, gt_f = jnp.split(mod, N_MOD, axis=-1)
        h = modulate(rms_norm(x, norm_mix_g[i]), sh_m, sc_m)
        j = i // N_MIXERS
        if i % N_MIXERS == 0:
            y = recurrent_mixer(h, lru_w_y[j], lru_b_y[j], lru_w_in[j], lru_b_in[j],
                                lru_conv_w[j], lru_conv_b[j], lru_w_a[j], lru_b_a[j],
                                lru_w_x[j], lru_b_x[j], lru_lambda[j], lru_w_out[j], lru_b_out[j])
        else:
            y = pool_mixer(h, pool_w[j], pool_scale[j])
        x = x + gt_m[:, None, :] * y
        h = modulate(rms_norm(x, norm_ffn_g[i]), sh_f, sc_f)
        x = x + gt_f[:, None, :] * sq_relu_mlp(h, ffn_w1[i], ffn_w2[i])
    return rms_norm(x, final_norm_g)


GRID_W = 64
HEAD_DIM = 64

NA_HEADS = 6
NA_WIN_H = 8
NA_WIN_W = 16
A_WIDTH = NA_HEADS * HEAD_DIM

MLA_HEADS = 6
MLA_Q_RANK = 256
MLA_KV_RANK = 128
MLA_NOPE = 64
MLA_ROPE = 32
MLA_QK = MLA_NOPE + MLA_ROPE
MLA_V = 64
B_WIDTH = MLA_HEADS * MLA_V
ROPE_THETA = 10000.0
Q_BLOCK = 128

CONV_GROUPS = 4
CONV_CH = CONV_GROUPS * HEAD_DIM
CONV_W = 3
C_WIDTH = CONV_CH

D_MIX = A_WIDTH + B_WIDTH + C_WIDTH
IN_SIZES = (A_WIDTH, A_WIDTH, A_WIDTH, MLA_Q_RANK, MLA_KV_RANK, MLA_ROPE, C_WIDTH, C_WIDTH, C_WIDTH)
IN_COLS = sum(IN_SIZES)

N_EXPERTS = 16
EXPERT_FF = 1024
CAPACITY_FACTOR = 2


def rms_norm_2(x, g):
    xf = x.astype(jnp.float32)
    y = xf * lax.rsqrt(jnp.mean(xf * xf, axis=-1, keepdims=True) + EPS)
    return (y * g.astype(jnp.float32)).astype(x.dtype)

def rope(x, pos):
    half = x.shape[-1] // 2
    inv = ROPE_THETA ** (-jnp.arange(half, dtype=jnp.float32) / half)
    ang = pos.astype(jnp.float32)[:, None] * inv[None, :]
    cos = jnp.cos(ang)[None, :, None, :]
    sin = jnp.sin(ang)[None, :, None, :]
    xf = x.astype(jnp.float32)
    x1, x2 = xf[..., :half], xf[..., half:]
    return jnp.concatenate([x1 * cos - x2 * sin, x2 * cos + x1 * sin], axis=-1).astype(x.dtype)

def neighbourhood_attention(q, k, v, rpb):
    b, s, h, dh = q.shape
    rows = s // GRID_W
    wh = min(NA_WIN_H, rows)
    ww = NA_WIN_W
    cols = np.arange(GRID_W)
    col_idx = np.clip(cols - ww // 2, 0, GRID_W - ww)[:, None] + np.arange(ww)[None, :]
    col_off = col_idx - cols[:, None] + (NA_WIN_W - 1)
    qg = q.reshape(b, rows, GRID_W, h, dh).transpose(1, 0, 2, 3, 4)
    kg = k.reshape(b, rows, GRID_W, h, dh)
    vg = v.reshape(b, rows, GRID_W, h, dh)
    scale = dh ** -0.5

    def one_row(args):
        r, q_row = args
        r0 = jnp.clip(r - wh // 2, 0, rows - wh)
        k_win = lax.dynamic_slice_in_dim(kg, r0, wh, axis=1)[:, :, col_idx]
        v_win = lax.dynamic_slice_in_dim(vg, r0, wh, axis=1)[:, :, col_idx]
        row_off = r0 + jnp.arange(wh) - r + (NA_WIN_H - 1)
        bias = rpb[:, row_off[:, None, None], col_off[None, :, :]].transpose(0, 2, 1, 3)
        sc = jnp.einsum('bqhd,biqjhd->bhqij', q_row, k_win).astype(jnp.float32) * scale
        sc = sc + bias.astype(jnp.float32)[None]
        p = jax.nn.softmax(sc.reshape(b, h, GRID_W, wh * ww), axis=-1).reshape(sc.shape).astype(v.dtype)
        return jnp.einsum('bhqij,biqjhd->bqhd', p, v_win)

    o = lax.map(one_row, (jnp.arange(rows), qg))
    return o.transpose(1, 0, 2, 3, 4).reshape(b, s, h * dh)

def mla_attention(q, k, v):
    b, s, h, dq = q.shape
    dv = v.shape[-1]
    nblk = s // Q_BLOCK
    scale = dq ** -0.5
    qb = q.reshape(b, nblk, Q_BLOCK, h, dq).transpose(1, 0, 2, 3, 4)

    def one_block(q_blk):
        sc = jnp.einsum('bqhd,bkhd->bhqk', q_blk, k).astype(jnp.float32) * scale
        p = jax.nn.softmax(sc, axis=-1).astype(v.dtype)
        return jnp.einsum('bhqk,bkhd->bqhd', p, v)

    o = lax.map(one_block, qb)
    return o.transpose(1, 0, 2, 3, 4).reshape(b, s, h * dv)

def short_conv_mixer(hc, bc, cc, conv_w):
    u = cc * hc
    y = lax.conv_general_dilated(
        u, conv_w[:, None, :].astype(u.dtype), window_strides=(1,),
        padding=((CONV_W // 2, CONV_W // 2),), dimension_numbers=('NWC', 'WIO', 'NWC'),
        feature_group_count=u.shape[-1])
    return bc * y

def expert_choice_moe(x, w_router, b_router, w_gate, w_up, w_down):
    b, s, d = x.shape
    cap = CAPACITY_FACTOR * s // N_EXPERTS
    logits = jnp.einsum('bsd,de->bse', x, w_router).astype(jnp.float32) + b_router.astype(jnp.float32)
    aff = jax.nn.softmax(logits, axis=-1)
    gate, idx = lax.top_k(aff.transpose(0, 2, 1), cap)
    bidx = jnp.arange(b)[:, None, None]
    xs = x[bidx, idx]
    hid = jax.nn.silu(jnp.einsum('becd,edf->becf', xs, w_gate)) * jnp.einsum('becd,edf->becf', xs, w_up)
    ys = jnp.einsum('becf,efd->becd', hid, w_down) * gate[..., None].astype(x.dtype)
    return jnp.zeros_like(x).at[bidx, idx].add(ys)

def hybrid_layer(x, pos, norm_mix, w_in, q_norm_a, k_norm_a, rpb, cq_norm, w_uq, ckv_norm, w_ukv,
                 q_norm_b, k_norm_b, conv_w, out_norm, w_out, norm_ffn, w_router, b_router,
                 w_gate, w_up, w_down):
    b, s, _ = x.shape
    hn = rms_norm_2(x, norm_mix)
    proj = jnp.einsum('bsd,dc->bsc', hn, w_in)
    splits = np.cumsum(IN_SIZES)[:-1].tolist()
    qa, ka, va, cq, ckv, kr, hc, bc, cc = jnp.split(proj, splits, axis=-1)

    qa = rms_norm_2(qa.reshape(b, s, NA_HEADS, HEAD_DIM), q_norm_a)
    ka = rms_norm_2(ka.reshape(b, s, NA_HEADS, HEAD_DIM), k_norm_a)
    va = va.reshape(b, s, NA_HEADS, HEAD_DIM)
    out_a = neighbourhood_attention(qa, ka, va, rpb)

    qb = jnp.einsum('bsr,rc->bsc', rms_norm_2(cq, cq_norm), w_uq).reshape(b, s, MLA_HEADS, MLA_QK)
    kv = jnp.einsum('bsr,rc->bsc', rms_norm_2(ckv, ckv_norm), w_ukv).reshape(b, s, MLA_HEADS, MLA_NOPE + MLA_V)
    kb = jnp.concatenate(
        [kv[..., :MLA_NOPE], jnp.broadcast_to(kr[:, :, None, :], (b, s, MLA_HEADS, MLA_ROPE))], axis=-1)
    vb = kv[..., MLA_NOPE:]
    qb = rms_norm_2(qb, q_norm_b)
    kb = rms_norm_2(kb, k_norm_b)
    qb = jnp.concatenate([qb[..., :MLA_NOPE], rope(qb[..., MLA_NOPE:], pos)], axis=-1)
    kb = jnp.concatenate([kb[..., :MLA_NOPE], rope(kb[..., MLA_NOPE:], pos)], axis=-1)
    out_b = mla_attention(qb, kb, vb)

    out_c = short_conv_mixer(hc, bc, cc, conv_w)

    mixed = jnp.concatenate([
        rms_norm_2(out_a, out_norm[:A_WIDTH]),
        rms_norm_2(out_b, out_norm[A_WIDTH:A_WIDTH + B_WIDTH]),
        rms_norm_2(out_c, out_norm[A_WIDTH + B_WIDTH:]),
    ], axis=-1)
    x = x + jnp.einsum('bsc,cd->bsd', mixed, w_out)
    x = x + expert_choice_moe(rms_norm_2(x, norm_ffn), w_router, b_router, w_gate, w_up, w_down)
    return x

def second_inputs(seed: int = 0) -> dict:
    key = jax.random.key(seed)
    ks = jax.random.split(key, 22)
    f32 = jnp.float32

    def nrm(k, shape, scale):
        return jax.random.normal(k, shape, f32) * scale

    def gain(k, shape):
        return 1.0 + 0.05 * jax.random.normal(k, shape, f32)

    res_scale = (2 * DEPTH) ** -0.5
    return {
        'x': nrm(ks[0], (BATCH, SEQ, D_MODEL), 1.0),
        'norm_mix': gain(ks[1], (DEPTH, D_MODEL)),
        'w_in': nrm(ks[2], (DEPTH, D_MODEL, IN_COLS), D_MODEL ** -0.5),
        'q_norm_a': gain(ks[3], (DEPTH, HEAD_DIM)),
        'k_norm_a': gain(ks[4], (DEPTH, HEAD_DIM)),
        'rpb': nrm(ks[5], (DEPTH, NA_HEADS, 2 * NA_WIN_H - 1, 2 * NA_WIN_W - 1), 0.1),
        'cq_norm': gain(ks[6], (DEPTH, MLA_Q_RANK)),
        'w_uq': nrm(ks[7], (DEPTH, MLA_Q_RANK, MLA_HEADS * MLA_QK), MLA_Q_RANK ** -0.5),
        'ckv_norm': gain(ks[8], (DEPTH, MLA_KV_RANK)),
        'w_ukv': nrm(ks[9], (DEPTH, MLA_KV_RANK, MLA_HEADS * (MLA_NOPE + MLA_V)), MLA_KV_RANK ** -0.5),
        'q_norm_b': gain(ks[10], (DEPTH, MLA_QK)),
        'k_norm_b': gain(ks[11], (DEPTH, MLA_QK)),
        'conv_w': nrm(ks[12], (DEPTH, CONV_W, CONV_CH), CONV_W ** -0.5),
        'out_norm': gain(ks[13], (DEPTH, D_MIX)),
        'w_out': nrm(ks[14], (DEPTH, D_MIX, D_MODEL), D_MIX ** -0.5 * res_scale),
        'norm_ffn': gain(ks[15], (DEPTH, D_MODEL)),
        'w_router': nrm(ks[16], (DEPTH, D_MODEL, N_EXPERTS), D_MODEL ** -0.5),
        'b_router': nrm(ks[17], (DEPTH, N_EXPERTS), 0.01),
        'w_gate': nrm(ks[18], (DEPTH, N_EXPERTS, D_MODEL, EXPERT_FF), D_MODEL ** -0.5),
        'w_up': nrm(ks[19], (DEPTH, N_EXPERTS, D_MODEL, EXPERT_FF), D_MODEL ** -0.5),
        'w_down': nrm(ks[20], (DEPTH, N_EXPERTS, EXPERT_FF, D_MODEL), EXPERT_FF ** -0.5),
    }

def second_block(x, norm_mix, w_in, q_norm_a, k_norm_a, rpb, cq_norm, w_uq, ckv_norm, w_ukv,
              q_norm_b, k_norm_b, conv_w, out_norm, w_out, norm_ffn, w_router, b_router,
              w_gate, w_up, w_down):
    pos = jnp.arange(x.shape[1], dtype=jnp.int32)
    for l in range(DEPTH):
        x = hybrid_layer(x, pos, norm_mix[l], w_in[l], q_norm_a[l], k_norm_a[l], rpb[l], cq_norm[l],
                         w_uq[l], ckv_norm[l], w_ukv[l], q_norm_b[l], k_norm_b[l], conv_w[l],
                         out_norm[l], w_out[l], norm_ffn[l], w_router[l], b_router[l],
                         w_gate[l], w_up[l], w_down[l])
    return x


def setup_inputs(seed=0):
    out = dict(first_inputs(seed))
    for name, value in second_inputs(seed + 1).items():
        if name != "x":
            out[name + "_2"] = value
    return out


def reference(
    x, c, w_mod, b_mod, norm_mix_g, norm_ffn_g, lru_w_y, lru_b_y, lru_w_in, lru_b_in,
    lru_conv_w, lru_conv_b, lru_w_a, lru_b_a, lru_w_x, lru_b_x, lru_lambda, lru_w_out,
    lru_b_out, pool_w, pool_scale, ffn_w1, ffn_w2, final_norm_g, norm_mix_2, w_in_2, q_norm_a_2,
    k_norm_a_2, rpb_2, cq_norm_2, w_uq_2, ckv_norm_2, w_ukv_2, q_norm_b_2, k_norm_b_2, conv_w_2,
    out_norm_2, w_out_2, norm_ffn_2, w_router_2, b_router_2, w_gate_2, w_up_2, w_down_2,
):
    x = first_block(
        x, c, w_mod, b_mod, norm_mix_g, norm_ffn_g, lru_w_y, lru_b_y, lru_w_in, lru_b_in,
        lru_conv_w, lru_conv_b, lru_w_a, lru_b_a, lru_w_x, lru_b_x, lru_lambda, lru_w_out,
        lru_b_out, pool_w, pool_scale, ffn_w1, ffn_w2, final_norm_g,
    )
    return second_block(
        x, norm_mix_2, w_in_2, q_norm_a_2, k_norm_a_2, rpb_2, cq_norm_2, w_uq_2, ckv_norm_2,
        w_ukv_2, q_norm_b_2, k_norm_b_2, conv_w_2, out_norm_2, w_out_2, norm_ffn_2, w_router_2,
        b_router_2, w_gate_2, w_up_2, w_down_2,
    )


_drawn_inputs = setup_inputs


def setup_inputs(seed=0):
    import zlib

    import numpy as np

    out = dict(_drawn_inputs(seed))
    spreads = {}
    factors = {'lru_b_y': 3.88,
     'lru_b_in': 2.736,
     'lru_conv_b': 2.758,
     'lru_b_a': 8.0,
     'lru_b_x': 8.0,
     'lru_b_out': 3.597,
     'q_norm_a_2': 4.64,
     'k_norm_a_2': 5.401,
     'cq_norm_2': 4.184,
     'q_norm_b_2': 4.882,
     'k_norm_b_2': 4.885,
     'b_router_2': 5.633}
    for name, (base, spread) in spreads.items():
        noise = np.random.default_rng([zlib.crc32(name.encode()), seed]).standard_normal(out[name].shape)
        drawn = base * np.exp(spread * noise) if base else spread * noise
        out[name] = jnp.asarray(drawn.astype(out[name].dtype))
    for name, factor in factors.items():
        out[name] = (out[name] * factor).astype(out[name].dtype)
    return out
```

```python
from contextlib import ExitStack

import concourse.bass as bass
from concourse import mybir

F32 = mybir.dt.float32
U32 = mybir.dt.uint32
ACT = mybir.ActivationFunctionType
ALU = mybir.AluOpType
AX = mybir.AxisListType

P = 128
D = 1024
S = 512
KC = D // P
TC = S // P
FF = 4096
FC = FF // P
DEPTH = 2
EPS = 1e-6
WINDOWS = (2, 4, 8, 16)
PAD = 16
GRID = 64
NA_HEADS, HD = 6, 64
A_W = NA_HEADS * HD
RPB_H, RPB_W = 15, 31
TOEP = 2 * GRID - 1
B_HEADS, QK, NOPE, ROPE, VD = 6, 96, 64, 32, 64
QR, KVR = 256, 128
CONV = 256
EXPERTS, CAP, EFF = 16, 64, 1024
SLOT = 4096
GELU_C = 0.7978845608028654
VROWS = 35
DVE_LAYER = 169
NVEC = 11 + 3 + DEPTH * 10

ROW_A = dict(norm_mix_g=0, norm_ffn_g=16, lru_b_y=32, lru_b_in=40, lru_conv_w=48, lru_conv_b=80,
             lru_b_a=88, lru_b_x=96, lru_lambda=104, lru_b_out=112, pool_scale=120)
B_MOD, B_FINAL, B_C, B_ROWS = 0, 96, 104, 112
G_MIX, G_FFN, G_OUT, G_CQ, G_CKV, G_CONV, G_QA, G_KA = 0, 8, 16, 24, 26, 27, 33, 34

C_ID, C_FLIP, C_MASK, C_COS, C_SIN, C_INV, C_N = 0, 128, 256, 320, 384, 448, 512


class Chain:

    def __init__(self, eng, sem):
        self.eng, self.sem, self.n, self.loops = eng, sem, 0, []

    def value(self):
        v = self.n
        for reg, per in self.loops:
            v = reg * per + v
        return v

    def __call__(self, ins):
        self.n += 1
        ins.then_inc(self.sem, 1)
        self.eng.wait_ge(self.sem, self.value())

    def enter(self, reg, per):
        self.loops.append((reg, per))
        return self.n

    def leave(self, n0, count):
        reg, per = self.loops.pop()
        assert self.n - n0 == per, (self.n - n0, per)
        self.n = n0 + per * count


class Settle:

    def __init__(self, eng, sem):
        self.eng, self.sem = eng, sem

    def __call__(self):
        self.eng.sem_inc(self.sem, 1)

    def wait_ge(self, sem, value):
        self.eng.wait_ge(sem, value)
        if not isinstance(value, int):
            self()


def R1_IN(s, f):
    if s:
        return 16 * (f + 1)
    return 16 * (f + 1) + (112 if f >= 2 else 0) + (48 if f >= 7 else 0)


def one(ap):
    return ap.rearrange("p a n -> p (a n)")


def program(nc, a, out):
    with ExitStack() as ctx:
        def sb(name, shape, dt=F32):
            return ctx.enter_context(nc.sbuf_tensor(name, shape, dt))

        def sem(name):
            return ctx.enter_context(nc.semaphore(name))

        arena = sb("arena", [P, 50176])

        def at(lo, n, pat=None, **kw):
            v = arena[:, lo:lo + n]
            return v.rearrange(pat, **kw) if pat else v

        ps = ctx.enter_context(nc.psum_tensor("ps", [P, 8, 512], F32))
        const = sb("const", [P, C_N])
        ident, flip = const[:, C_ID:C_ID + P], const[:, C_FLIP:C_FLIP + P]
        ones = sb("ones", [P, P])
        vrow = sb("vrow", [P, 3, P])
        vA = sb("vA", [P, P])
        vB = sb("vB", [P, B_ROWS])
        v2 = sb("v2", [P, DEPTH * VROWS])
        modc = sb("modc", [P, 96])
        small = sb("small", [P, 16, 8])
        qkg = sb("qkg", [P, 2, DEPTH, QK])
        wr = sb("wr", [P, DEPTH, KC, EXPERTS])
        br = sb("br", [P, DEPTH, EXPERTS])
        ring1 = [at(SLOT * s, SLOT) for s in range(4)]
        big = 16384
        gelu_b = at(big, 4096, "p (k n) -> p k n", k=KC)
        xr = at(big + 4096, KC * 515, "p (k n) -> p k n", k=KC)
        xc = at(big + 4096 + 4120, 4096, "p (k n) -> p k n", k=KC)
        u2 = at(big, 16384, "p (k n) -> p k n", k=FC)
        x_rows = at(big, 4096, "p (t d) -> p t d", t=TC)
        hp = at(big, KC * (PAD + S), "p (k n) -> p k n", k=KC)
        pw = [at(big + 4224 + 1056 * i, 1056, "p (k n) -> p k n", k=2) for i in range(2)]
        acc0 = [at(big + 4096 + 1024 * i, 1024) for i in range(2)]
        xT = at(32768, 4096, "p (k n) -> p k n", k=KC)
        hT = at(36864, 4096, "p (k n) -> p k n", k=KC)
        squares = [hT if u % 2 == 0 else at(big + 12288, 4096, "p (k n) -> p k n", k=KC) for u in range(5)]
        mod_in = [at(40960 + 1024 * i, 1024) for i in range(2)]
        mod_acc = [at(43008 + 1024 * i, 1024) for i in range(2)]
        mod_t = at(45056, 1024)
        tmp = [at(46080 + 512 * i, 512) for i in range(8)]
        ring2 = [at(SLOT * s, SLOT) for s in range(6)]
        x_tok = at(24576, 4096, "p (t d) -> p t d", t=TC)
        hnT = at(28672, 4096, "p (k n) -> p k n", k=KC)
        R = 32768
        xn = at(R, 4096, "p (t d) -> p t d", t=TC)
        bias = [at(28672 + 1778 * i, 1778, "p (r n) -> p r n", r=14) for i in range(2)]
        qk = at(R, 3072, "p (t d) -> p t d", t=TC)
        va = at(R + 3072, 1536, "p (t d) -> p t d", t=TC)
        qb = at(R + 4608, 2304, "p (t h d) -> p t h d", t=TC, h=B_HEADS)
        kb = at(R + 6912, 2304, "p (t h d) -> p t h d", t=TC, h=B_HEADS)
        vb = at(R + 9216, 1536, "p (t d) -> p t d", t=TC)
        oc = at(R + 10752, 1024, "p (k n) -> p k n", k=2)
        W = R + 11776
        cv = at(W, 3072, "p (k n) -> p k n", k=6)
        cu = at(W + 3072, 1028, "p (k n) -> p k n", k=2)
        cvs = at(W + 4100, 1024, "p (k n) -> p k n", k=2)
        p3 = at(W, 1664, "p (t d) -> p t d", t=TC)
        p3sq = at(W + 1664, 1536, "p (t d) -> p t d", t=TC)
        cT = at(W + 3200, 1536, "p (k n) -> p k n", k=3)
        normsq = at(W, 3072)
        ropet = [at(W + 384 * i, 384, "p (t h d) -> p t h d", t=TC, h=B_HEADS) for i in range(4)]
        stage_q = at(W, 768, "p (t h d) -> p t h d", t=TC, h=2)
        stage_k = at(W + 768, 768, "p (t h d) -> p t h d", t=TC, h=2)
        stage_qa = at(W, 512, "p (t d) -> p t d", t=TC)
        stage_ka = at(W + 768, 512, "p (t d) -> p t d", t=TC)
        qT = at(W + 1536, 1024, "p (h n) -> p h n", h=2)
        kT = at(W + 2560, 1024, "p (h n) -> p h n", h=2)
        prob = at(W + 3584, 1024, "p (b n) -> p b n", b=2)
        probT = at(W + 4608, 1024, "p (b n) -> p b n", b=2)
        mix_sq = at(W, 1536, "p (t h d) -> p t h d", t=TC, h=6)
        mix_tok = at(W + 1536, 3072, "p (t c) -> p t c", t=TC)
        lg = at(R + 4096, 64, "p (t e) -> p t e", t=TC)
        st = sb("st", [P, 160])
        aff = at(R + 4160, 512)
        aff2 = at(R + 4672, 512)
        top_v = at(R + 5184, 128)
        top_i = at(R + 5312, 64).bitcast(U32)
        idx_f = at(R + 5376, 192)
        gate_t = at(R + 5568, 16)
        put_i = at(R + 5584, 16).bitcast(U32)
        get_i = at(R + 5600, 16).bitcast(U32)
        get_c = [sb(f"get_c{i}", [CAP, 1], U32) for i in range(2)]
        put_c = [sb(f"put_c{i}", [P, 1], U32) for i in range(2)]
        xg = [at(R + 5632 + 1024 * i, 1024) for i in range(2)]
        xsT = [at(R + 7680 + 512 * i, 512, "p (k n) -> p k n", k=KC) for i in range(2)]
        hid = [at(R + 8704 + 512 * i, 512) for i in range(2)]
        hidt = [at(R + 9728 + 512 * i, 512) for i in range(2)]
        hT2 = [at(R + 10752 + 512 * i, 512, "p (k n) -> p k n", k=4) for i in range(2)]
        ye = [at(R + 11776 + 512 * i, 512) for i in range(2)]
        toep = nc.dram_tensor("toep", (DEPTH, NA_HEADS * RPB_H * TOEP), F32, kind="Internal").ap()
        xn_dram = nc.dram_tensor("xn_rows", (S, D), F32, kind="Internal").ap()
        toep_sb = at(46080 + 3072, 2 * TOEP + 2, "p (l n) -> p l n", l=2)
        out_t = out.rearrange("b (t p) d -> p (b t) d", p=P)
        out_rows = out.rearrange("b t (h d) -> (b t h) d", h=2)

        names = """const_in vec_in x_in toep_zero rpb_in toep_out
          vec_T vec_cols xr_T x_done cond_t cond mod_sum mod_ps mod_cols
          sq_done ss_done inv_done rstd_done hn_part h_done
          lam_abs lam_exp lru_const
          y_ps y_sb y_sq y_arg y_tanh xi_ps xi_sb conv_done
          gate_ps gate_act gate_free neg_done sqrt_done z_done wo_ps
          f1_ps relu_done u_free f2_ps pool_done wp_ps fin_done fin_T x_ready
          n_ss n_inv n_rstd xn_done xt_ps hn_ready gains_in
          proj_ps proj_copied conv_ps conv_copied conv_sq cs_ps c_inv c_rstd
          c_ss c_r c_normed ct_ps ct_copied p2_ps p2_copied qk_ss qk_r qk_normed
          staged st_T st_copied bias_ready bias_used s_ps s_max p_done pt_ps pt_copied o_ps o_done
          m_ss m_r m_normed mt_ps mt_copied mix67 wout_ps x_added acc_saved xn_saved
          lg_ps lg_max lg_exp aff_done aff_ps idx_done idx_ps idx_cols
          xst_ps xs_ready g_ps g_tanh u_ps hid_done ht_ps ht_copied y2_ps ye_done
          dve_step pool_step gain_done settled get_col put_col fin_copied stage_free put_free gains_set kr_copied""".split()
        sm = {n: sem(n) for n in names}
        r1_in = [sem(f"ring1_in{s}") for s in range(4)]
        r1_used = [sem(f"ring1_used{s}") for s in range(4)]
        r2_in = [sem(f"ring2_in{s}") for s in range(6)]
        r2_used = [sem(f"ring2_used{s}") for s in range(6)]
        mod_in_s = [sem(f"mod_in{i}") for i in range(2)]
        bias_in = [sem(f"bias_in{i}") for i in range(2)]
        got = [sem(f"rows_got{i}") for i in range(2)]
        put = [sem(f"rows_put{i}") for i in range(2)]
        F_FFN = ([3, 3, 3, 2], [8, 7, 7, 6])
        O_FFN = (0, 1)
        R1_FILLS = (12, 11, 11, 10)
        USES = [17, 17, 17, 17, 18, 18]

        R2_IN = [288, 288, 288, 272, 288, 288]
        R2_BASE = [48, 48, 48, 32, 48, 48]

        block = ctx.enter_context(nc.Block())

        @block.sync
        def _(sp):
            sp.dma_start(const[:, :], a["consts"]).then_inc(sm["const_in"], 16)
            sp.dma_start(x_rows, a["x"].rearrange("b (t p) d -> p (b t) d", p=P)).then_inc(sm["x_in"], 16)
            fills = [0, 0, 0, 0]
            settle = Settle(sp, sm["settled"])

            def fill(s, dst, src):
                if fills[s] >= 1:
                    sp.wait_ge(r1_used[s], fills[s])
                fills[s] += 1
                sp.dma_start(dst, src).then_inc(r1_in[s], 16)

            def k_rows(w, c0, c1, k0=0, k1=KC):
                return w.rearrange("(k p) n -> p k n", p=P)[:, k0:k1, c0:c1]

            def slot(s, k):
                return ring1[s].rearrange("p (k n) -> p k n", k=k)

            for m in range(4):
                j, half = divmod(m, 2)
                fill(m, slot(m, 4), k_rows(a["w_mod"][0], j * D, (j + 1) * D, 4 * half, 4 * half + 4))
            for i in range(2):
                fill(i, slot(i, KC), k_rows(a["lru_w_y"][0], 512 * i, 512 * i + 512))
            for i in range(2):
                fill(2 + i, slot(2 + i, KC), k_rows(a["lru_w_in"][0], 512 * i, 512 * i + 512))
            for n, w in enumerate(("lru_w_a", "lru_w_x")):
                if n == 0:
                    sp.wait_ge(r1_used[0], fills[0])
                    fills[0] += 1
                for h in range(4):
                    sp.dma_start(ring1[0][:, n * 2048 + h * 512:n * 2048 + h * 512 + 512]
                                 .rearrange("p (i n) -> p i n", i=2),
                                 a[w][0, h].rearrange("(i p) n -> p i n", p=P)).then_inc(r1_in[0], 16)
            for i in range(2):
                fill(1 + i, slot(1 + i, KC), k_rows(a["lru_w_out"][0], 512 * i, 512 * i + 512))

            def ffn(l):
                f0, o = F_FFN[l], O_FFN[l]
                settle()
                with sp.Fori(0, 2) as i:
                    for b in range(4):
                        s = (o + b) % 4
                        sp.wait_ge(r1_used[s], i + f0[s])
                        sp.dma_start(slot(s, KC), a["ffn_w1"][l].rearrange("(k p) n -> p k n", p=P)
                                     [:, :, bass.ds(i * 2048 + 512 * b, 512)]).then_inc(r1_in[s], 16)
                settle()
                with sp.Fori(0, 2) as i:
                    for b in range(4):
                        s = (o + b) % 4
                        sp.wait_ge(r1_used[s], i + (f0[s] + 2))
                        sp.dma_start(slot(s, FC), a["ffn_w2"][l].rearrange("(k p) n -> p k n", p=P)
                                     [:, :, bass.ds(i * 512 + P * b, P)]).then_inc(r1_in[s], 16)

            ffn(0)
            sp.wait_ge(r1_used[0], 7)
            for g in range(4):
                sp.dma_start(ring1[0][:, g * 512:g * 512 + 512].rearrange("p (i n) -> p i n", i=2),
                             a["pool_w"][0, g].rearrange("(i p) n -> p i n", p=P)).then_inc(r1_in[0], 16)
            ffn(1)

            for s in range(4):
                sp.wait_ge(r1_used[s], R1_FILLS[s])
            sp.wait_ge(sm["x_done"], 40)
            with sp.Fori(0, DEPTH) as l:
                w_in = a["w_in_2"][bass.ds(l, 1)].rearrange("a (k p) n -> p (a k) n", p=P)
                edge = [0, 384, 768, 1152, 1568, 1952, 2336]
                for s in range(6):
                    n = edge[s + 1] - edge[s]
                    sp.wait_ge(r2_used[s], l * USES[s] + 1)
                    sp.dma_start(ring2[s][:, 0:KC * n].rearrange("p (k n) -> p k n", k=KC),
                                 w_in[:, :, edge[s]:edge[s + 1]]).then_inc(r2_in[s], 16)
                uq = a["w_uq_2"][bass.ds(l, 1)].rearrange("a (k p) n -> p (a k) n", p=P)
                sp.dma_start(ring2[0][:, 3072:3840],
                             a["w_ukv_2"][bass.ds(l, 1)].rearrange("a p n -> (a p) n")).then_inc(r2_in[0], 16)
                for i in range(2):
                    sp.dma_start(ring2[1 + i][:, 3072:3648], uq[:, i, :]).then_inc(r2_in[1 + i], 16)
                w_out = a["w_out_2"][bass.ds(l, 1)].rearrange("a (k p) n -> p (a k) n", p=P)
                for s in (4, 5):
                    sp.wait_ge(r2_used[s], l * USES[s] + 2)
                    sp.dma_start(ring2[s].rearrange("p (k n) -> p k n", k=4),
                                 w_out[:, 4 * (s - 4):4 * (s - 4) + 4, :]).then_inc(r2_in[s], 16)

                def bias_tiles(h, i):
                    src = toep[bass.ds(l, 1), bass.ds(h * (RPB_H * TOEP), RPB_H * TOEP)]
                    for q in range(2):
                        view = bass.AP(src.tensor, src.offset + (1 - q) * TOEP, [[1, GRID], [1, 13 * TOEP + GRID]])
                        sp.dma_start(bias[i][q * GRID:(q + 1) * GRID].rearrange("p r n -> p (r n)")
                                     [:, 0:13 * TOEP + GRID], view).then_inc(bias_in[i], 16)

                sp.wait_ge(sm["toep_out"], 32)
                sp.wait_ge(sm["conv_ps"], l * 6 + 6)
                sp.wait_ge(sm["proj_ps"], l * 16 + 16)
                settle()
                with sp.Fori(0, 3) as p:
                    for i in range(2):
                        sp.wait_ge(sm["bias_used"], l * 6 + p * 2 + (i + 1))
                        bias_tiles(p * 2 + i, i)

                settle()
                with sp.Fori(0, EXPERTS) as e:
                    for n, w in enumerate(("w_gate_2", "w_up_2", "w_down_2")):
                        we = a[w][bass.ds(l, 1), bass.ds(e, 1)].rearrange("a b (k p) n -> p (a b k) n", p=P)
                        for i in range(2):
                            s = 2 * n + i
                            sp.wait_ge(r2_used[s], l * USES[s] + e + (2 if s < 4 else 3))
                            sp.dma_start(ring2[s].rearrange("p (k n) -> p k n", k=4),
                                         we[:, 4 * i:4 * i + 4, :]).then_inc(r2_in[s], 16)

        @block.scalar
        def _(act):
            settle = Settle(act, sm["settled"])

            def A(out, in_, *args, **kw):
                if settling:
                    settle()
                return nc.scalar.activation(out, in_, *args, **kw)

            settling = []
            act.sem_inc(sm["bias_used"], 2)
            act.sem_inc(sm["u_free"], 4)
            act.sem_inc(sm["gate_free"], 2)
            act.sem_inc(sm["put_free"], 2)
            act.sem_inc(sm["stage_free"], 1)
            for s in range(6):
                act.sem_inc(r2_used[s], 1)
            nvec = 0
            for n, r in ROW_A.items():
                v = a[n]
                v = v.rearrange("a (r p) -> (a r) p", p=P) if len(v.shape) == 2 else \
                    v.rearrange("a b (r p) -> (a b r) p", p=P)
                act.dma_start(vrow[r:r + v.shape[0], 0, :], v).then_inc(sm["vec_in"], 16)
                nvec += 1
            act.dma_start(vrow[0:96, 1, :], a["b_mod"].rearrange("a (r p) -> (a r) p", p=P)).then_inc(sm["vec_in"], 16)
            act.dma_start(vrow[96:104, 1, :], a["final_norm_g"].rearrange("(r p) -> r p", p=P)).then_inc(sm["vec_in"], 16)
            act.dma_start(vrow[104:112, 1, :], a["c"].rearrange("a (r p) -> (a r) p", p=P)).then_inc(sm["vec_in"], 16)
            nvec += 3
            for l in range(DEPTH):
                o = l * VROWS
                for n, r, k in (("norm_mix_2", G_MIX, 8), ("norm_ffn_2", G_FFN, 8), ("out_norm_2", G_OUT, 8),
                                ("cq_norm_2", G_CQ, 2), ("ckv_norm_2", G_CKV, 1)):
                    act.dma_start(vrow[o + r:o + r + k, 2, :],
                                  a[n][l].rearrange("(r p) -> r p", p=P)).then_inc(sm["vec_in"], 16)
                act.dma_start(vrow[o + G_CONV:o + G_CONV + 6, 2, :],
                              a["conv_w_2"][l].rearrange("w (r p) -> (w r) p", p=P)).then_inc(sm["vec_in"], 16)
                nvec += 6
                for n, r in (("q_norm_a_2", G_QA), ("k_norm_a_2", G_KA)):
                    for i in range(2):
                        act.dma_start(vrow[o + r:o + r + 1, 2, HD * i:HD * i + HD],
                                      a[n][l:l + 1, :]).then_inc(sm["vec_in"], 16)
                        nvec += 1
            assert nvec == NVEC

            act.wait_ge(sm["vec_cols"], 2)
            A(small[:, 0, :], vB[:, B_C:B_C + 8], ACT.Tanh, scale=0.5).then_inc(sm["cond_t"], 1)
            A(small[:, 1, :], vA[:, 104:112], ACT.Abs).then_inc(sm["lam_abs"], 1)
            act.wait_ge(sm["lam_abs"], 1)
            A(small[:, 2, :], small[:, 1, :], ACT.Exp, scale=-1.0).then_inc(sm["lam_exp"], 1)
            A(small[:, 3, :], vA[:, 88:96], ACT.Copy, scale=0.5).then_inc(sm["lru_const"], 1)
            A(small[:, 4, :], vA[:, 96:104], ACT.Copy, scale=0.5).then_inc(sm["lru_const"], 1)

            def second_tables():
                for l in range(DEPTH):
                    act.dma_start(wr[:, l, :, :], a["w_router_2"][l].rearrange("(k p) e -> p k e", p=P)).then_inc(sm["gains_in"], 16)
                    act.dma_start(br[:, l, :], a["b_router_2"][l:l + 1, :].partition_broadcast(P)).then_inc(sm["gains_in"], 16)
                    for i, n in enumerate(("q_norm_b_2", "k_norm_b_2")):
                        act.dma_start(qkg[:, i, l, :], a[n][l:l + 1, :].partition_broadcast(P)).then_inc(sm["gains_in"], 16)
                act.wait_ge(sm["toep_zero"], 1)
                for l in range(DEPTH):
                    act.dma_start(toep_sb[0:90, l, GRID - RPB_W // 2 - 1:GRID - RPB_W // 2 - 1 + RPB_W],
                                  a["rpb_2"][l].rearrange("h r c -> (h r) c")).then_inc(sm["rpb_in"], 16)
                act.wait_ge(sm["rpb_in"], 32)
                for l in range(DEPTH):
                    act.dma_start(toep[l].rearrange("(r c) -> r c", c=TOEP), toep_sb[0:90, l, 0:TOEP]).then_inc(sm["toep_out"], 16)

            def norm(u):
                for k in range(KC):
                    act.wait_ge(sm["x_done"], 8 * u + k + 1)
                    A(squares[u][:, k, :], xT[:, k, :], ACT.Square).then_inc(sm["sq_done"], 1)
                act.wait_ge(sm["inv_done"], u + 1)
                A(tmp[1], tmp[0], ACT.Sqrt).then_inc(sm["rstd_done"], 1)
                if u == 4:
                    return
                l, g, sh = u // 2, 5 + u, (0, 3)[u % 2]
                for k in range(KC):
                    act.wait_ge(sm["hn_part"], 8 * u + k + 1)
                    dst = hp[:, k, PAD:] if u == 2 else hT[:, k, :]
                    A(dst, hT[:, k, :], ACT.Identity, scale=small[:, g, k:k + 1],
                      bias=modc[:, l * 48 + sh * 8 + k:l * 48 + sh * 8 + k + 1]).then_inc(sm["h_done"], 1)

            norm(0)
            second_tables()

            settling.append(1)
            with act.Fori(0, 2) as i:
                for b in range(4):
                    c, t = i * 4 + b, tmp[2 + b % 2]
                    act.wait_ge(sm["y_ps"], c + 1)
                    A(one(gelu_b[:, bass.ds(c, 1), :]), ps[:, b, :], ACT.Identity,
                      bias=vA[:, bass.ds(c + 32, 1)]).then_inc(sm["y_sb"], 1)
                    act.wait_ge(sm["y_sb"], c + 1)
                    A(t, one(gelu_b[:, bass.ds(c, 1), :]), ACT.Square).then_inc(sm["y_sq"], 1)
                    act.wait_ge(sm["y_arg"], c + 1)
                    A(t, t, ACT.Tanh, scale=GELU_C).then_inc(sm["y_tanh"], 1)
            for s in range(2):
                act.sem_inc(r1_used[s], 1)
            with act.Fori(0, 2) as i:
                for b in range(4):
                    c = i * 4 + b
                    act.wait_ge(sm["xi_ps"], c + 1)
                    A(one(xr[:, bass.ds(c, 1), 3:515]), ps[:, b, :], ACT.Identity,
                      bias=vA[:, bass.ds(c + 40, 1)]).then_inc(sm["xi_sb"], 1)
            for s in (2, 3):
                act.sem_inc(r1_used[s], 1)
            act.wait_ge(sm["conv_done"], 8)
            act.wait_ge(sm["lru_const"], 3)
            with act.Fori(0, 4) as h:
                for j in range(2):
                    c = h * 2 + j
                    act.wait_ge(sm["gate_ps"], c + 1)
                    act_t = tmp[2 + j]
                    n0 = c * 3
                    A(act_t, ps[:, 2 * j, :], ACT.Tanh, scale=0.5, bias=small[:, 3, bass.ds(c, 1)]).then_inc(sm["gate_act"], 1)
                    act.wait_ge(sm["gate_act"], n0 + 1)
                    A(one(xr[:, bass.ds(c, 1), 0:512]), act_t, ACT.Tanh, scale=small[:, 10, bass.ds(c, 1)],
                      bias=small[:, 10, bass.ds(c, 1)]).then_inc(sm["gate_act"], 1)
                    act.wait_ge(sm["gate_free"], c + 1)
                    A(tmp[4 + j], ps[:, 2 * j + 1, :], ACT.Tanh, scale=0.5, bias=small[:, 4, bass.ds(c, 1)]).then_inc(sm["gate_act"], 1)
            act.sem_inc(r1_used[0], 1)
            act.wait_ge(sm["neg_done"], 8)
            with act.Fori(0, KC) as c:
                A(one(xr[:, bass.ds(c, 1), 0:512]), one(xr[:, bass.ds(c, 1), 0:512]), ACT.Sqrt).then_inc(sm["sqrt_done"], 1)

            settling.clear()

            def ffn(l):
                with act.Fori(0, 2) as i:
                    for b in range(4):
                      for j in range(4):
                        c = i * 16 + (4 * b + j)
                        act.wait_ge(sm["f1_ps"], c + (l * 32 + 1))
                        if j == 3:
                            act.sem_inc(r1_used[(O_FFN[l] + b) % 4], 1)
                        act.wait_ge(sm["u_free"], c + (l * 32 + 3))
                        A(tmp[2 + j % 2], ps[:, j, :], ACT.Relu).then_inc(sm["relu_done"], 1)

            norm(1)
            ffn(0)
            norm(2)
            norm(3)
            ffn(1)
            norm(4)

            act.wait_ge(sm["toep_out"], 32)
            with act.Fori(0, DEPTH) as l:
                act.wait_ge(sm["x_ready"], l * 16 + 16)
                gain = st[:, 96:96 + VROWS]
                A(gain, v2[:, bass.ds(l * VROWS, VROWS)], ACT.Copy).then_inc(sm["gains_set"], 1)
                act.wait_ge(sm["gains_set"], l + 1)

                def norm2(w):
                    for t in range(TC):
                        if w == 1:
                            act.wait_ge(sm["x_added"], l * 8 + (2 * t + 2))
                        A(xn[:, t, :], x_tok[:, t, :], ACT.Square, accum_out=st[:, t:t + 1]).then_inc(sm["n_ss"], 1)
                    act.wait_ge(sm["n_inv"], l * 2 + (w + 1))
                    A(st[:, 8:12], st[:, 4:8], ACT.Sqrt).then_inc(sm["n_rstd"], 1)
                    for k in range(KC):
                        act.wait_ge(sm["xt_ps"], l * 16 + (8 * w + k + 1))
                        A(hnT[:, k, :], ps[:, 4 + k % 2, :], ACT.Copy,
                          scale=gain[:, (G_MIX, G_FFN)[w] + k:(G_MIX, G_FFN)[w] + k + 1]).then_inc(sm["hn_ready"], 1)

                norm2(0)
                for j, dst in enumerate((qk[:, :, 0:384], qk[:, :, 384:768], va, p3)):
                    for t in range(TC):
                        act.wait_ge(sm["proj_ps"], l * 16 + (4 * j + t + 1))
                        n = dst.shape[2]
                        A(dst[:, t, :], ps[:, t, 0:n], ACT.Copy).then_inc(sm["proj_copied"], 1)
                act.wait_ge(sm["c_ss"], l + 1)
                A(st[:, 24:32], st[:, 16:24], ACT.Sqrt).then_inc(sm["c_r"], 1)
                for i in range(3):
                    act.wait_ge(sm["ct_ps"], l * 3 + (i + 1))
                    A(cT[:, i, :], ps[:, 4 + i, :], ACT.Copy, scale=gain[:, G_CQ + i:G_CQ + i + 1]).then_inc(sm["ct_copied"], 1)
                for t in range(TC):
                    for i in range(2):
                        act.wait_ge(sm["p2_ps"], l * 16 + (4 * t + i + 1))
                        A(qb[:, t, 3 * i:3 * i + 3, :], ps[:, i, 0:288].rearrange("p (h d) -> p h d", h=3), ACT.Copy) \
                            .then_inc(sm["p2_copied"], 1)
                    for i in range(2):
                        act.wait_ge(sm["p2_ps"], l * 16 + (4 * t + i + 3))
                        kv = ps[:, 2 + i, 0:384].rearrange("p (h d) -> p h d", h=3)
                        A(kb[:, t, 3 * i:3 * i + 3, 0:NOPE], kv[:, :, 0:NOPE], ACT.Copy)
                        A(vb[:, t, 192 * i:192 * i + 192].rearrange("p (h d) -> p h d", h=3), kv[:, :, NOPE:], ACT.Copy) \
                            .then_inc(sm["p2_copied"], 1)
                act.wait_ge(sm["p2_ps"], l * 16 + 16)
                act.wait_ge(sm["kr_copied"], l + 1)
                for c in range(6):
                    act.wait_ge(sm["conv_ps"], l * 6 + (c + 1))
                    A(cv[:, c, :], ps[:, 4 + c % 4, :], ACT.Copy).then_inc(sm["conv_copied"], 1)
                act.wait_ge(sm["c_inv"], l + 1)
                A(cvs[:, 1, :], cvs[:, 0, :], ACT.Sqrt).then_inc(sm["c_rstd"], 1)
                for i in range(2):
                    act.wait_ge(sm["qk_ss"], l * 2 + (i + 1))
                    A(st[:, 48:96], st[:, 48:96], ACT.Sqrt).then_inc(sm["qk_r"], 1)

                def heads(kind):
                    with act.Fori(0, 3) as p:
                        for i in range(2 if kind == 0 else 4):
                            act.wait_ge(sm["st_T"], l * 18 + p * (2, 4)[kind] + ((0, 6)[kind] + i + 1))
                            if kind == 0:
                                A((qT, kT)[i][:, 0, :], ps[:, 4 + i, :], ACT.Copy,
                                  scale=gain[:, G_QA + i:G_QA + i + 1]).then_inc(sm["st_copied"], 1)
                            else:
                                A((qT, kT)[i // 2][0:QK, i % 2, :], ps[0:QK, 4 + i % 2, :], ACT.Copy).then_inc(sm["st_copied"], 1)
                        act.sem_inc(sm["stage_free"], 1)
                        for i in range(9):
                            n = l * 48 + p * 8 + kind * 24
                            if i < 8:
                                act.wait_ge(sm["s_max"], n + (i + 1))
                                src = prob[:, i % 2, :] if kind == 0 else ps[:, i % 2, :]
                                A(prob[:, i % 2, :], src, ACT.Exp, bias=st[:, 32 + i:33 + i],
                                  scale=(1.0, QK ** -0.5)[kind], accum_out=st[:, 40 + i:41 + i]).then_inc(sm["p_done"], 1)
                            if i >= 1:
                                act.wait_ge(sm["pt_ps"], n + i)
                                if i >= 3:
                                    act.wait_ge(sm["o_ps"], n + (i - 2))
                                A(probT[:, (i - 1) % 2, :], ps[:, 2 + (i - 1) % 2, :], ACT.Copy).then_inc(sm["pt_copied"], 1)

                heads(0)
                heads(1)
                act.wait_ge(sm["m_ss"], l + 1)
                A(st[:, 16:24], st[:, 16:24], ACT.Sqrt).then_inc(sm["m_r"], 1)
                for c in range(6):
                    act.wait_ge(sm["mt_ps"], l * 6 + (c + 1))
                    A(hnT[:, c, :], ps[:, 4 + c % 2, :], ACT.Copy, scale=gain[:, G_OUT + c:G_OUT + c + 1]).then_inc(sm["mt_copied"], 1)
                norm2(1)
                act.dma_start(out_t, x_tok).then_inc(sm["acc_saved"], 16)
                act.wait_ge(sm["xn_done"], l * 8 + 8)
                act.dma_start(xn_dram.rearrange("(t p) d -> p t d", p=P), xn).then_inc(sm["xn_saved"], 16)
                act.wait_ge(sm["lg_max"], l + 1)
                A(lg.rearrange("p t e -> p (t e)"), lg.rearrange("p t e -> p (t e)"), ACT.Exp).then_inc(sm["lg_exp"], 1)
                with act.Fori(0, EXPERTS // 2) as i:
                    for b in range(2):
                        n = l * 16 + i * 2 + b
                        act.wait_ge(sm["g_ps"], n + 1)
                        act.sem_inc(r2_used[1], 1)
                        A(hidt[b], ps[:, 2 * b, :], ACT.Tanh, scale=0.5).then_inc(sm["g_tanh"], 1)
                        act.wait_ge(sm["ht_ps"], n + 1)
                        A(hT2[b].rearrange("p k n -> p (k n)"), ps[:, 4, :], ACT.Copy).then_inc(sm["ht_copied"], 1)
                act.wait_ge(sm["put_free"], l * 16 + 18)
                act.dma_start(x_tok, out_t).then_inc(sm["x_ready"], 16)
            act.wait_ge(sm["x_ready"], 48)

        @block.vector
        def _(dve):
            V = nc.vector
            chain = Chain(dve, sm["dve_step"])
            settle = Settle(dve, sm["settled"])
            mul, add, sub = ALU.mult, ALU.add, ALU.subtract

            chain(V.memset(ones[:, :], 1.0))
            V.memset(toep_sb[:, :, :], 0.0).then_inc(sm["toep_zero"], 1)
            for i, (dst, n) in enumerate(((vA, P), (vB, B_ROWS), (v2, DEPTH * VROWS))):
                dve.wait_ge(sm["vec_T"], i + 1)
                V.tensor_copy(dst[:, :], ps[:, 4 + i, 0:n]).then_inc(sm["vec_cols"], 1)
            for k in range(KC):
                dve.wait_ge(sm["xr_T"], k + 1)
                V.tensor_copy(xT[:, k, :], ps[:, k % 4, :]).then_inc(sm["x_done"], 1)
            dve.wait_ge(sm["vec_cols"], 3)
            dve.wait_ge(sm["cond_t"], 1)
            cond = small[:, 5 + 8, :]
            chain(V.scalar_tensor_tensor(small[:, 14, :], small[:, 0, :], 1.0, vB[:, B_C:B_C + 8], add, mul))
            V.tensor_scalar(cond, small[:, 14, :], 0.5, None, mul).then_inc(sm["cond"], 1)
            dve.wait_ge(sm["cond"], 1)
            dve.wait_ge(sm["lam_exp"], 1)
            e, z, z2, q = small[:, 2, :], small[:, 11, :], small[:, 12, :], small[:, 14, :]
            chain(V.tensor_scalar(z, e, 2.0, None, add))
            chain(V.reciprocal(z, z))
            chain(V.tensor_tensor(z, z, e, mul))
            chain(V.tensor_tensor(z2, z, z, mul))
            chain(V.tensor_scalar(q, z2, 1.0 / 15, None, mul))
            for n in (13, 11, 9, 7, 5, 3):
                chain(V.scalar_tensor_tensor(q, q, 1.0 / n, z2, add, mul))
            chain(V.scalar_tensor_tensor(q, q, 1.0, z, add, mul))
            chain(V.tensor_scalar(z2, vA[:, 104:112], -1.0, 0.0, mul, ALU.max))
            chain(V.scalar_tensor_tensor(z, q, 2.0, z2, mul, add))
            V.tensor_scalar(small[:, 10, :], z, -2.0, None, mul).then_inc(sm["lru_const"], 1)

            for j in range(2):
                for half in range(2):
                    dve.wait_ge(r1_in[2 * j + half], 16)
                    w = ring1[2 * j + half].rearrange("p (k n) -> p k n", k=4)
                    for kk in range(4):
                        k = 4 * half + kk
                        if k == 0:
                            ins = V.tensor_scalar(acc0[j], w[:, kk, :], cond[:, 0:1], None, mul)
                        else:
                            ins = V.scalar_tensor_tensor(acc0[j], w[:, kk, :], cond[:, k:k + 1], acc0[j], mul, add)
                        if kk == 3:
                            ins.then_inc(r1_used[2 * j + half], 1)
                            dve.wait_ge(r1_used[2 * j + half], 1)
                        else:
                            chain(ins)

            def mod_columns(n):
                l, j = divmod(n, 6)
                dve.wait_ge(sm["mod_ps"], n + 1)
                V.tensor_tensor(modc[:, 8 * n:8 * n + 8], ps[:, 7, 8 * n:8 * n + 8], vB[:, 8 * n:8 * n + 8], add) \
                    .then_inc(sm["mod_cols"], 1)
                if j in (1, 4):
                    dve.wait_ge(sm["mod_cols"], n + 1)
                    u = 2 * l + (j == 4)
                    g = (0, 16)[j == 4] + 8 * l
                    V.scalar_tensor_tensor(small[:, 5 + u, :], modc[:, 8 * n:8 * n + 8], 1.0, vA[:, g:g + 8], add, mul) \
                        .then_inc(sm["gain_done"], 1)

            def norm(u):
                dve.wait_ge(sm["ss_done"], u + 1)
                chain(V.tensor_scalar(tmp[0], ps[:, 6, :], 1.0 / D, EPS, mul, add))
                V.reciprocal(tmp[0], tmp[0]).then_inc(sm["inv_done"], 1)
                dve.wait_ge(sm["rstd_done"], u + 1)
                for k in range(KC):
                    if u < 4:
                        V.tensor_tensor(hT[:, k, :], xT[:, k, :], tmp[1], mul).then_inc(sm["hn_part"], 1)
                    else:
                        V.scalar_tensor_tensor(hT[:, k, :], xT[:, k, :], vB[:, B_FINAL + k:B_FINAL + k + 1],
                                               tmp[1], mul, mul).then_inc(sm["fin_done"], 1)

            mod_columns(0)
            mod_columns(1)
            dve.wait_ge(sm["gain_done"], 1)
            V.memset(xr[:, :, 0:3], 0.0)
            norm(0)

            with dve.Fori(0, 2) as i:
                n0 = chain.enter(i, 4)
                for b in range(4):
                    c, t = i * 4 + b, tmp[2 + b % 2]
                    g = one(gelu_b[:, bass.ds(c, 1), :])
                    dve.wait_ge(sm["y_sq"], c + 1)
                    chain(V.tensor_scalar(t, t, 0.044715, 1.0, mul, add))
                    V.tensor_tensor(t, t, g, mul).then_inc(sm["y_arg"], 1)
                    dve.wait_ge(sm["y_tanh"], c + 1)
                    V.scalar_tensor_tensor(g, t, 1.0, g, add, mul)
                chain.leave(n0, 2)
            mod_columns(2)
            mod_columns(3)
            with dve.Fori(0, KC) as c:
                n0 = chain.enter(c, 3)
                dve.wait_ge(sm["xi_sb"], c + 1)
                o = one(xc[:, bass.ds(c, 1), :])
                chain(V.tensor_scalar(o, one(xr[:, bass.ds(c, 1), 0:512]), vA[:, bass.ds(c + 48, 1)],
                                      vA[:, bass.ds(c + 80, 1)], mul, add))
                for w in range(1, 4):
                    ins = V.scalar_tensor_tensor(o, one(xr[:, bass.ds(c, 1), w:w + 512]), vA[:, bass.ds(c + (48 + 8 * w), 1)],
                                                 o, mul, add)
                    if w < 3:
                        chain(ins)
                    else:
                        ins.then_inc(sm["conv_done"], 1)
                chain.leave(n0, KC)
            mod_columns(4)
            mod_columns(5)
            dve.wait_ge(sm["conv_done"], 8)
            with dve.Fori(0, 4) as h:
                n0 = chain.enter(h, 6)
                for j in range(2):
                    c = h * 2 + j
                    T = one(xr[:, bass.ds(c, 1), 0:512])
                    v = one(hT[:, bass.ds(c, 1), :])
                    dve.wait_ge(sm["gate_ps"], h * 2 + 2)
                    dve.wait_ge(sm["gate_act"], c * 3 + 3)
                    V.scalar_tensor_tensor(v, tmp[4 + j], 1.0, one(xc[:, bass.ds(c, 1), :]), add, mul) \
                        .then_inc(sm["gate_free"], 1)
                    dve.wait_ge(sm["gate_free"], c + 3)
                    chain(V.tensor_scalar(tmp[0], T, -1.0, 1.0, mul, add))
                    chain(V.reciprocal(tmp[0], tmp[0]))
                    V.tensor_tensor(v, v, tmp[0], mul)
                    chain(V.scalar_tensor_tensor(one(xc[:, bass.ds(c, 1), :]), T, 1.0, tmp[0], add, mul))
                    V.tensor_scalar(T, T, -1.0, 1e-30, mul, ALU.max).then_inc(sm["neg_done"], 1)
                chain.leave(n0, 4)
            with dve.Fori(0, KC) as c:
                n0 = chain.enter(c, 2)
                h, v = one(xr[:, bass.ds(c, 1), 0:512]), one(hT[:, bass.ds(c, 1), :])
                dve.wait_ge(sm["sqrt_done"], c + 1)
                chain(V.tensor_tensor(v, v, h, mul))
                chain(V.tensor_tensor_scan(h, one(xc[:, bass.ds(c, 1), :]), v, 0.0, mul, add))
                V.scalar_tensor_tensor(v, h, 0.5, one(gelu_b[:, bass.ds(c, 1), :]), mul, mul).then_inc(sm["z_done"], 1)
                chain.leave(n0, KC)
            for c in range(KC):
                dve.wait_ge(sm["wo_ps"], c + 1)
                t = tmp[2 + c % 2]
                chain(V.tensor_scalar(t, ps[:, c % 4, :], vA[:, 112 + c:113 + c], modc[:, 16 + c:17 + c], add, mul))
                V.tensor_tensor(xT[:, c, :], xT[:, c, :], t, add).then_inc(sm["x_done"], 1)

            for s in (1, 2):
                dve.sem_inc(r1_used[s], 1)

            def ffn(l):
                with dve.Fori(0, 8) as i:
                    for j in range(4):
                        c = i * 4 + j
                        dve.wait_ge(sm["relu_done"], c + (32 * l + 1))
                        V.tensor_tensor(one(u2[:, bass.ds(c, 1), :]), tmp[2 + j % 2], ps[:, j, :], mul).then_inc(sm["u_free"], 1)
                if l == 0:
                    mod_columns(8)
                    mod_columns(9)
                with dve.Fori(0, 2) as i:
                    for b in range(4):
                        c = i * 4 + b
                        x = one(xT[:, bass.ds(c, 1), :])
                        dve.wait_ge(sm["f2_ps"], c + (8 * l + 1))
                        dve.sem_inc(r1_used[(O_FFN[l] + b) % 4], 1)
                        V.scalar_tensor_tensor(x, ps[:, b, :], modc[:, bass.ds(c + (48 * l + 40), 1)], x, mul, add) \
                            .then_inc(sm["x_done"], 1)

            norm(1)
            mod_columns(6)
            mod_columns(7)
            ffn(0)
            mod_columns(10)
            mod_columns(11)
            chain(V.tensor_tensor(small[:, 9, :], modc[:, 64:72], vA[:, 120:128], mul))
            V.memset(hp[:, :, 0:PAD], 0.0)
            for i in range(2):
                V.memset(pw[i][:, :, 0:PAD], 0.0)
            norm(2)
            for g, win in enumerate(WINDOWS):
                dve.wait_ge(sm["h_done"], 16 + 2 * g + 2)
                if g >= 1:
                    dve.wait_ge(sm["pool_done"], g)
                src = x0 = hp[:, 2 * g:2 * g + 2, :]
                w, n = 1, 0
                while w < win:
                    dst = pw[n % 2]
                    chain(V.tensor_tensor(dst[:, :, PAD:], src[:, :, PAD:], src[:, :, PAD - w:PAD + S - w], add))
                    src, w, n = dst, 2 * w, n + 1
                inv = const[:, C_INV + 16 * g:C_INV + 16 * g + 16].unsqueeze(1).to_broadcast([P, 2, 16])
                V.scalar_tensor_tensor(hT[:, 2 * g:2 * g + 2, 16:], src[:, :, PAD + 16:], 1.0 / win,
                                       x0[:, :, PAD + 16:], mul, sub)
                chain(V.tensor_tensor(src[:, :, PAD:PAD + 16], src[:, :, PAD:PAD + 16], inv, mul))
                V.tensor_tensor(hT[:, 2 * g:2 * g + 2, 0:16], src[:, :, PAD:PAD + 16], x0[:, :, PAD:PAD + 16], sub) \
                    .then_inc(sm["pool_done"], 1)
            for c in range(KC):
                dve.wait_ge(sm["wp_ps"], c + 1)
                V.scalar_tensor_tensor(xT[:, c, :], ps[:, c % 4, :], small[:, 9, c:c + 1], xT[:, c, :], mul, add) \
                    .then_inc(sm["x_done"], 1)
            dve.sem_inc(r1_used[0], 1)
            norm(3)
            ffn(1)
            norm(4)
            for t in range(TC):
                for half in range(2):
                    n = 2 * t + half
                    dve.wait_ge(sm["fin_T"], n + 1)
                    ins = V.tensor_copy(x_tok[:, t, 512 * half:512 * half + 512], ps[:, n % 4, :])
                    ins.then_inc(sm["fin_copied"], 1)
            dve.wait_ge(sm["fin_copied"], 8)
            chain(V.memset(st[:, 156:157], 0.0))
            V.tensor_copy(st[:, 157:158], st[:, 156:157]).then_inc(sm["x_ready"], 16)

            with dve.Fori(0, DEPTH) as l:
                c0 = chain.enter(l, DVE_LAYER)
                gain = st[:, 96:96 + VROWS]

                def norm2(w):
                    dve.wait_ge(sm["n_ss"], l * 8 + (4 * w + 4))
                    chain(V.tensor_scalar(st[:, 4:8], st[:, 0:4], 1.0 / D, EPS, mul, add))
                    V.reciprocal(st[:, 4:8], st[:, 4:8]).then_inc(sm["n_inv"], 1)
                    dve.wait_ge(sm["n_rstd"], l * 2 + (w + 1))
                    for t in range(TC):
                        V.tensor_scalar(xn[:, t, :], x_tok[:, t, :], st[:, 8 + t:9 + t], None, mul).then_inc(sm["xn_done"], 1)

                norm2(0)
                dve.wait_ge(sm["proj_copied"], l * 16 + 16)
                chain(V.tensor_tensor(p3sq, p3[:, :, 0:384], p3[:, :, 0:384], mul))
                V.tensor_reduce(st[:, 16:20], p3sq[:, :, 0:QR], AX.X, add)
                chain(V.tensor_reduce(st[:, 20:24], p3sq[:, :, QR:], AX.X, add))
                V.tensor_scalar(st[:, 16:20], st[:, 16:20], 1.0 / QR, EPS, mul, add)
                chain(V.tensor_scalar(st[:, 20:24], st[:, 20:24], 1.0 / KVR, EPS, mul, add))
                V.reciprocal(st[:, 16:24], st[:, 16:24]).then_inc(sm["c_ss"], 1)
                dve.wait_ge(sm["c_r"], l + 1)
                for t in range(TC):
                    V.tensor_scalar(p3[:, t, 0:QR], p3[:, t, 0:QR], st[:, 24 + t:25 + t], None, mul)
                    V.tensor_scalar(p3[:, t, QR:384], p3[:, t, QR:384], st[:, 28 + t:29 + t], None, mul).then_inc(sm["c_normed"], 1)
                for h in range(B_HEADS):
                    ins = V.tensor_copy(kb[:, :, h, NOPE:], p3[:, :, 384:416])
                ins.then_inc(sm["kr_copied"], 1)

                dve.wait_ge(sm["conv_copied"], l * 6 + 6)
                V.memset(cu[:, :, 0:1], 0.0)
                V.memset(cu[:, :, 513:514], 0.0)
                chain(V.tensor_tensor(cu[:, :, 1:513], cv[:, 4:6, :], cv[:, 0:2, :], mul))
                for j in range(2):
                    w = [gain[:, G_CONV + 2 * k + j:G_CONV + 2 * k + j + 1] for k in range(3)]
                    chain(V.tensor_scalar(oc[:, j, :], cu[:, j, 0:512], w[0], None, mul))
                    chain(V.scalar_tensor_tensor(oc[:, j, :], cu[:, j, 1:513], w[1], oc[:, j, :], mul, add))
                    chain(V.scalar_tensor_tensor(oc[:, j, :], cu[:, j, 2:514], w[2], oc[:, j, :], mul, add))
                chain(V.tensor_tensor(oc, oc, cv[:, 2:4, :], mul))
                V.tensor_tensor(cvs, oc, oc, mul).then_inc(sm["conv_sq"], 1)
                dve.wait_ge(sm["cs_ps"], l + 1)
                chain(V.tensor_scalar(cvs[:, 0, :], ps[:, 4, :], 1.0 / CONV, EPS, mul, add))
                V.reciprocal(cvs[:, 0, :], cvs[:, 0, :]).then_inc(sm["c_inv"], 1)
                dve.wait_ge(sm["c_rstd"], l + 1)
                for j in range(2):
                    V.scalar_tensor_tensor(oc[:, j, :], oc[:, j, :], gain[:, G_OUT + 6 + j:G_OUT + 7 + j],
                                           cvs[:, 1, :], mul, mul)

                qa12 = qk.rearrange("p t (h d) -> p (t h) d", d=HD)
                chain(V.tensor_tensor(normsq, qk.rearrange("p t d -> p (t d)"), qk.rearrange("p t d -> p (t d)"), mul))
                chain(V.tensor_reduce(st[:, 48:96], normsq.rearrange("p (h d) -> p h d", d=HD), AX.X, add))
                chain(V.tensor_scalar(st[:, 48:96], st[:, 48:96], 1.0 / HD, EPS, mul, add))
                V.reciprocal(st[:, 48:96], st[:, 48:96]).then_inc(sm["qk_ss"], 1)
                dve.wait_ge(sm["qk_r"], l * 2 + 1)
                chain(V.tensor_tensor(qa12, qa12, st[:, 48:96].unsqueeze(2).to_broadcast([P, 48, HD]), mul))
                dve.wait_ge(sm["p2_copied"], l * 16 + 16)
                sq = normsq[:, 0:2304]
                for i, x in enumerate((qb, kb)):
                    flat = x.rearrange("p t h d -> p (t h d)")
                    chain(V.tensor_tensor(sq, flat, flat, mul))
                    chain(V.tensor_reduce(st[:, 48 + 24 * i:72 + 24 * i], sq.rearrange("p (h d) -> p h d", d=QK), AX.X, add))
                chain(V.tensor_scalar(st[:, 48:96], st[:, 48:96], 1.0 / QK, EPS, mul, add))
                V.reciprocal(st[:, 48:96], st[:, 48:96]).then_inc(sm["qk_ss"], 1)
                dve.wait_ge(sm["qk_r"], l * 2 + 2)
                for i, x in enumerate((qb, kb)):
                    v = x.rearrange("p t h d -> p (t h) d")
                    chain(V.tensor_tensor(v, v, st[:, 48 + 24 * i:72 + 24 * i].unsqueeze(2).to_broadcast([P, 24, QK]), mul))
                    g = qkg[:, i, bass.ds(l, 1), :].to_broadcast([P, 24, QK])
                    chain(V.tensor_tensor(v, v, g, mul))
                    x1, x2 = x[:, :, :, NOPE:NOPE + 16], x[:, :, :, NOPE + 16:]
                    cos = const[:, C_COS:C_COS + 64].rearrange("p (t n) -> p t n", t=TC).unsqueeze(2).to_broadcast([P, TC, B_HEADS, 16])
                    sin = const[:, C_SIN:C_SIN + 64].rearrange("p (t n) -> p t n", t=TC).unsqueeze(2).to_broadcast([P, TC, B_HEADS, 16])
                    V.tensor_tensor(ropet[0], x1, cos, mul)
                    V.tensor_tensor(ropet[1], x2, sin, mul)
                    V.tensor_tensor(ropet[2], x2, cos, mul)
                    chain(V.tensor_tensor(ropet[3], x1, sin, mul))
                    V.tensor_tensor(x1, ropet[0], ropet[1], sub)
                    ins = V.tensor_tensor(x2, ropet[2], ropet[3], add)
                    if i == 0:
                        chain(ins)
                    else:
                        ins.then_inc(sm["qk_normed"], 1)

                def heads(kind):
                    settle()
                    with dve.Fori(0, 3) as p:
                        n1 = chain.enter(p, 16)
                        n = l * 48 + p * 8 + kind * 24

                        def out_tile(i):
                            hh, t = divmod(i, 4)
                            dve.wait_ge(sm["o_ps"], n + (i + 1))
                            if kind == 0:
                                dst = one(qk[:, t:t + 1, bass.ds(p * 128 + 64 * hh, 64)])
                            else:
                                dst = one(qb[:, t, bass.ds(p * 2 + hh, 1), 0:VD])
                            V.tensor_scalar(dst, ps[:, 6 + i % 2, 0:64], st[:, 144 + i:145 + i], None, mul) \
                                .then_inc(sm["o_done"], 1)

                        for i in range(8):
                            hh, t = divmod(i, 4)
                            dve.wait_ge(sm["s_ps"], n + (i + 1))
                            if kind == 0:
                                if t == 0:
                                    dve.wait_ge(sm["bias_ready"], l * 6 + p * 2 + (hh + 1))
                                b = bias[hh][:, 6 - 2 * t:14 - 2 * t, 0:GRID]
                                sc = prob[:, i % 2, :].rearrange("p (r n) -> p r n", n=GRID)
                                ins = V.scalar_tensor_tensor(sc, ps[:, i % 2, :].rearrange("p (r n) -> p r n", n=GRID),
                                                             HD ** -0.5, b, mul, add)
                                chain(ins)
                                if t == 3:
                                    V.tensor_copy(st[:, 157:158], st[:, 156:157]).then_inc(sm["bias_used"], 1)
                                V.tensor_reduce(st[:, 32 + i:33 + i], prob[:, i % 2, :], AX.X, ALU.max, negate=True) \
                                    .then_inc(sm["s_max"], 1)
                            else:
                                chain(V.tensor_reduce(st[:, 32 + i:33 + i], ps[:, i % 2, :], AX.X, ALU.max, negate=True))
                                V.tensor_scalar(st[:, 32 + i:33 + i], st[:, 32 + i:33 + i], QK ** -0.5, None, mul) \
                                    .then_inc(sm["s_max"], 1)
                            if i >= 1:
                                dve.wait_ge(sm["p_done"], n + i)
                                chain(V.reciprocal(st[:, 143 + i:144 + i], st[:, 39 + i:40 + i]))
                            if i >= 3:
                                out_tile(i - 3)
                        dve.wait_ge(sm["p_done"], n + 8)
                        chain(V.reciprocal(st[:, 151:152], st[:, 47:48]))
                        for i in (5, 6, 7):
                            out_tile(i)
                        chain.leave(n1, 3)

                heads(0)
                heads(1)

                dve.wait_ge(sm["o_done"], l * 48 + 48)
                va_out = qk[:, :, 0:A_W].rearrange("p t (h d) -> p t h d", h=6)
                vb_out = qb[:, :, :, 0:VD]
                for i, x in enumerate((va_out, vb_out)):
                    chain(V.tensor_tensor(mix_sq, x, x, mul))
                    chain(V.tensor_reduce(st[:, 16 + 4 * i:20 + 4 * i], mix_sq.rearrange("p t h d -> p t (h d)"), AX.X, add))
                chain(V.tensor_scalar(st[:, 16:24], st[:, 16:24], 1.0 / A_W, EPS, mul, add))
                V.reciprocal(st[:, 16:24], st[:, 16:24]).then_inc(sm["m_ss"], 1)
                dve.wait_ge(sm["m_r"], l + 1)
                for i, x in enumerate((va_out, vb_out)):
                    for t in range(TC):
                        ins = V.tensor_scalar(mix_tok[:, t, A_W * i:A_W * i + A_W].rearrange("p (h d) -> p h d", h=6),
                                              x[:, t], st[:, 16 + 4 * i + t:17 + 4 * i + t], None, mul)
                    ins.then_inc(sm["m_normed"], 1)
                V.tensor_copy(hnT[:, 6:8, :], oc).then_inc(sm["mix67"], 1)
                for n in range(8):
                    t, half = divmod(n, 2)
                    x = x_tok[:, t, 512 * half:512 * half + 512]
                    dve.wait_ge(sm["wout_ps"], l * 8 + (n + 1))
                    V.tensor_tensor(x, x, ps[:, n % 4, :], add).then_inc(sm["x_added"], 1)
                norm2(1)

                dve.wait_ge(sm["lg_ps"], l + 1)
                b = br[:, bass.ds(l, 1), :].to_broadcast([P, TC, EXPERTS])
                chain(V.tensor_tensor(lg, ps[:, 6, 0:64].rearrange("p (t e) -> p t e", t=TC), b, add))
                chain(V.tensor_reduce(st[:, 12:16], lg, AX.X, ALU.max))
                V.tensor_tensor(lg, lg, st[:, 12:16].unsqueeze(2).to_broadcast([P, TC, EXPERTS]), sub).then_inc(sm["lg_max"], 1)
                dve.wait_ge(sm["lg_exp"], l + 1)
                chain(V.tensor_reduce(st[:, 12:16], lg, AX.X, add))
                chain(V.reciprocal(st[:, 12:16], st[:, 12:16]))
                V.tensor_tensor(lg, lg, st[:, 12:16].unsqueeze(2).to_broadcast([P, TC, EXPERTS]), mul).then_inc(sm["aff_done"], 1)
                dve.wait_ge(sm["aff_ps"], l + 1)
                chain(V.tensor_copy(aff[0:EXPERTS], ps[0:EXPERTS, 7, :]))
                for r in range(CAP // 8):
                    src, dst = (aff, aff2) if r % 2 == 0 else (aff2, aff)
                    v8 = top_v[0:EXPERTS, 8 * r:8 * r + 8]
                    settle()
                    chain(V.max(v8, src[0:EXPERTS]))
                    settle()
                    ins = V.max_index(top_i[0:EXPERTS, 8 * r:8 * r + 8], v8, src[0:EXPERTS])
                    if r < CAP // 8 - 1:
                        ins = V.match_replace(dst[0:EXPERTS], v8, src[0:EXPERTS], -1.0)
                    chain(ins)
                V.tensor_copy(top_v[0:EXPERTS, CAP:], top_v[0:EXPERTS, 0:CAP])
                chain(V.tensor_copy(idx_f[0:EXPERTS, 128:192], top_i[0:EXPERTS]))
                V.tensor_scalar(idx_f[0:EXPERTS, 0:64], idx_f[0:EXPERTS, 128:192], 2.0, None, mul)
                V.tensor_scalar(idx_f[0:EXPERTS, 64:128], idx_f[0:EXPERTS, 128:192], 2.0, 1.0, mul, add).then_inc(sm["idx_done"], 1)
                dve.wait_ge(sm["idx_ps"], l + 1)
                V.tensor_copy(gate_t, ps[:, 6, 64:80])
                V.tensor_copy(put_i, ps[:, 6, 80:96])
                V.tensor_copy(get_i[0:CAP], ps[0:CAP, 6, 96:112]).then_inc(sm["idx_cols"], 1)
                dve.wait_ge(sm["idx_cols"], l + 1)

                settle()
                with dve.Fori(0, EXPERTS // 2) as i:
                    n1 = chain.enter(i, 2)
                    for b in range(2):
                        n = l * 16 + i * 2 + b
                        dve.wait_ge(sm["xst_ps"], n + 1)
                        V.tensor_tensor(xsT[b], ps[:, 5, :].rearrange("p (k n) -> p k n", k=KC),
                                        gain[:, G_FFN:G_FFN + 8].unsqueeze(2).to_broadcast([P, KC, CAP]), mul) \
                            .then_inc(sm["xs_ready"], 1)
                        dve.wait_ge(sm["g_tanh"], n + 1)
                        chain(V.scalar_tensor_tensor(hid[b], hidt[b], 1.0, ps[:, 2 * b, :], add, mul))
                        dve.wait_ge(sm["u_ps"], n + 1)
                        dve.sem_inc(r2_used[3], 1)
                        V.scalar_tensor_tensor(hid[b], hid[b], 0.5, ps[:, 2 * b + 1, :], mul, mul).then_inc(sm["hid_done"], 1)
                        dve.wait_ge(sm["y2_ps"], n + 1)
                        dve.sem_inc(r2_used[5], 1)
                        dve.wait_ge(sm["put_free"], n + 1)
                        V.tensor_scalar(ye[b], ps[:, 6 + b, :], gate_t[:, bass.ds(i * 2 + b, 1)], None, mul) \
                            .then_inc(sm["ye_done"], 1)
                    chain.leave(n1, 8)
                chain.leave(c0, DEPTH)

        @block.tensor
        def _(pe):
            mm, tr = nc.tensor.matmul, nc.tensor.transpose
            settle = Settle(pe, sm["settled"])

            pe.wait_ge(sm["const_in"], 16)
            pe.wait_ge(sm["vec_in"], 16 * NVEC)
            for i, n in enumerate((P, B_ROWS, DEPTH * VROWS)):
                tr(ps[:, 4 + i, 0:n], vrow[0:n, i, :], ident[0:n, 0:n]).then_inc(sm["vec_T"], 1)
            pe.wait_ge(sm["x_in"], 16)
            for k in range(KC):
                if k >= 4:
                    pe.wait_ge(sm["x_done"], k - 3)
                for t in range(TC):
                    ins = tr(ps[:, k % 4, P * t:P * t + P], x_rows[:, t, P * k:P * k + P], ident)
                ins.then_inc(sm["xr_T"], 1)

            def mod_sum(n):
                src = acc0[n] if n < 2 else mod_acc[n % 2]
                if n >= 1:
                    pe.wait_ge(sm["mod_cols"], n)
                if n < 2:
                    pe.wait_ge(r1_used[2 * n + 1], 1)
                else:
                    pe.wait_ge(sm["mod_sum"], n - 1)
                for k in range(KC):
                    ins = mm(ps[:, 7, 8 * n + k:8 * n + k + 1], src[:, P * k:P * k + P], ones[:, 0:1], start=True, stop=True)
                ins.then_inc(sm["mod_ps"], 1)

            def norm(u):
                for k in range(KC):
                    pe.wait_ge(sm["sq_done"], 8 * u + k + 1)
                    ins = mm(ps[:, 6, :], ones[:, :], squares[u][:, k, :], start=(k == 0), stop=(k == KC - 1))
                ins.then_inc(sm["ss_done"], 1)

            def dense(name, slots, fill, u, freed, base=0):
                for c in range(KC):
                    s = slots[c // 4]
                    if c % 4 == 0:
                        pe.wait_ge(r1_in[s], 16 * (fill + 1))
                    if c >= 4:
                        pe.wait_ge(sm[freed], base + c - 3)
                    w = ring1[s].rearrange("p (k n) -> p k n", k=KC)
                    for k in range(KC):
                        if c == 0:
                            if u is None:
                                pe.wait_ge(sm["z_done"], k + 1)
                            else:
                                pe.wait_ge(sm["h_done"], 8 * u + k + 1)
                        ins = mm(ps[:, c % 4, :], w[:, k, P * (c % 4):P * (c % 4) + P], hT[:, k, :],
                                 start=(k == 0), stop=(k == KC - 1))
                    ins.then_inc(sm[name], 1)

            mod_sum(0)
            mod_sum(1)
            norm(0)
            dense("y_ps", (0, 1), 1, 0, "y_sb")
            mod_sum(2)
            mod_sum(3)
            pe.wait_ge(sm["y_sb"], 8)
            dense("xi_ps", (2, 3), 1, 0, "xi_sb")
            mod_sum(4)
            mod_sum(5)
            pe.wait_ge(r1_in[0], 32 + 16 * 8)
            pe.wait_ge(sm["xi_sb"], 8)
            wg = ring1[0].rearrange("p (g h i n) -> p g h i n", g=2, h=4, i=2)
            for c in range(KC):
                h, j = divmod(c, 2)
                pe.wait_ge(sm["conv_done"], 2 * h + 2)
                if c >= 2:
                    pe.wait_ge(sm["gate_act"], 3 * (c - 1))
                for g in range(2):
                    for i in range(2):
                        ins = mm(ps[:, 2 * (c % 2) + g, :], wg[:, g, h, i, P * j:P * j + P], xc[:, 2 * h + i, :],
                                 start=(i == 0), stop=(i == 1))
                ins.then_inc(sm["gate_ps"], 1)
            pe.wait_ge(sm["gate_act"], 24)
            dense("wo_ps", (1, 2), 2, None, "x_done", 8)

            def ffn(l):
                f0, o = F_FFN[l], O_FFN[l]
                pe.wait_ge(sm["h_done"], 8 * (2 * l + 2))
                with pe.Fori(0, 2) as i:
                    for b in range(4):
                        s = (o + b) % 4
                        pe.wait_ge(r1_in[s], i * 16 + R1_IN(s, f0[s]))
                        w = ring1[s].rearrange("p (k n) -> p k n", k=KC)
                        for j in range(4):
                            pe.wait_ge(sm["u_free"], i * 16 + (32 * l + 4 * b + j + 1))
                            for k in range(KC):
                                ins = mm(ps[:, j, :], w[:, k, P * j:P * j + P], hT[:, k, :], start=(k == 0), stop=(k == KC - 1))
                            ins.then_inc(sm["f1_ps"], 1)
                if l == 0:
                    mod_sum(8)
                    mod_sum(9)
                pe.wait_ge(sm["u_free"], 32 * l + 36)
                with pe.Fori(0, 2) as i:
                    for b in range(4):
                        s = (o + b) % 4
                        pe.wait_ge(r1_in[s], i * 16 + R1_IN(s, f0[s] + 2))
                        pe.wait_ge(sm["x_done"], i * 4 + (16 + 16 * l + b - 3))
                        w = ring1[s].rearrange("p (k n) -> p k n", k=FC)
                        for f in range(FC):
                            ins = mm(ps[:, b, :], w[:, f, :], u2[:, f, :], start=(f == 0), stop=(f == FC - 1))
                        ins.then_inc(sm["f2_ps"], 1)

            norm(1)
            mod_sum(6)
            mod_sum(7)
            ffn(0)
            mod_sum(10)
            mod_sum(11)
            norm(2)
            pe.wait_ge(r1_in[0], R1_IN(0, 7))
            wp = ring1[0][:, 0:2048].rearrange("p (g i n) -> p g i n", g=4, i=2)
            for c in range(KC):
                g, j = divmod(c, 2)
                pe.wait_ge(sm["pool_done"], g + 1)
                if c >= 4:
                    pe.wait_ge(sm["x_done"], 24 + c - 3)
                for i in range(2):
                    ins = mm(ps[:, c % 4, :], wp[:, g, i, P * j:P * j + P], hT[:, 2 * g + i, :], start=(i == 0), stop=(i == 1))
                ins.then_inc(sm["wp_ps"], 1)
            norm(3)
            ffn(1)
            norm(4)
            for t in range(TC):
                for half in range(2):
                    n = 2 * t + half
                    if n >= 4:
                        pe.wait_ge(sm["fin_copied"], n - 3)
                    for k in range(4):
                        pe.wait_ge(sm["fin_done"], 4 * half + k + 1)
                        ins = tr(ps[:, n % 4, P * k:P * k + P], hT[:, 4 * half + k, P * t:P * t + P], ident)
                    ins.then_inc(sm["fin_T"], 1)

            pe.wait_ge(sm["gains_in"], 16 * 8)
            with pe.Fori(0, DEPTH) as l:

                def norm2(w):
                    pe.wait_ge(sm["xn_done"], l * 8 + (4 * w + 4))
                    for k in range(KC):
                        if k >= 2:
                            pe.wait_ge(sm["hn_ready"], l * 16 + (8 * w + k - 1))
                        for t in range(TC):
                            ins = tr(ps[:, 4 + k % 2, P * t:P * t + P], xn[:, t, P * k:P * k + P], ident)
                        ins.then_inc(sm["xt_ps"], 1)

                def landed(s, n):
                    pe.wait_ge(r2_in[s], l * R2_IN[s] + 16 * n)

                def used(s, name, value):
                    pe.wait_ge(sm[name], value)
                    pe.sem_inc(r2_used[s], 1)

                norm2(0)
                pe.wait_ge(sm["hn_ready"], l * 16 + 8)
                for j in range(4):
                    n = 384 if j < 3 else 416
                    landed(j, 2 if j < 3 else 1)
                    w = ring2[j][:, 0:KC * n].rearrange("p (k n) -> p k n", k=KC)
                    for t in range(TC):
                        if j >= 1:
                            pe.wait_ge(sm["proj_copied"], l * 16 + (4 * j + t - 3))
                        for k in range(KC):
                            ins = mm(ps[:, t, 0:n], hnT[:, k, P * t:P * t + P], w[:, k, :], start=(k == 0), stop=(k == KC - 1))
                        ins.then_inc(sm["proj_ps"], 1)
                pe.wait_ge(sm["c_normed"], l * 4 + 4)
                for i in range(3):
                    for t in range(TC):
                        ins = tr(ps[:, 4 + i, P * t:P * t + P], p3[:, t, P * i:P * i + P], ident)
                    ins.then_inc(sm["ct_ps"], 1)
                pe.wait_ge(sm["ct_copied"], l * 3 + 3)
                for t in range(TC):
                    for i in range(4):
                        if t == 0:
                            pe.wait_ge(sm["proj_copied"], l * 16 + (13 + i))
                        else:
                            pe.wait_ge(sm["p2_copied"], l * 16 + (4 * t + i - 3))
                        if i < 2:
                            for k in range(2):
                                ins = mm(ps[:, i, 0:288], cT[:, k, P * t:P * t + P], ring2[1 + k][:, 3072 + 288 * i:3360 + 288 * i],
                                         start=(k == 0), stop=(k == 1))
                        else:
                            ins = mm(ps[:, i, 0:384], cT[:, 2, P * t:P * t + P], ring2[0][:, 3072 + 384 * (i - 2):3456 + 384 * (i - 2)],
                                     start=True, stop=True)
                        ins.then_inc(sm["p2_ps"], 1)
                for c in range(6):
                    s, j = 4 + c // 3, c % 3
                    if j == 0:
                        landed(s, 1)
                    if c >= 4:
                        pe.wait_ge(sm["conv_copied"], l * 6 + (c - 3))
                    w = ring2[s][:, 0:3072].rearrange("p (k n) -> p k n", k=KC)
                    for k in range(KC):
                        ins = mm(ps[:, 4 + c % 4, :], w[:, k, P * j:P * j + P], hnT[:, k, :], start=(k == 0), stop=(k == KC - 1))
                    ins.then_inc(sm["conv_ps"], 1)
                pe.wait_ge(sm["conv_sq"], l + 1)
                for s, name, value in ((3, "proj_ps", l * 16 + 16), (0, "p2_ps", l * 16 + 16), (1, "p2_ps", l * 16 + 16),
                                       (2, "p2_ps", l * 16 + 16), (4, "conv_ps", l * 6 + 6), (5, "conv_ps", l * 6 + 6)):
                    used(s, name, value)
                for j in range(2):
                    ins = mm(ps[:, 4, :], ones[:, :], cvs[:, j, :], start=(j == 0), stop=(j == 1))
                ins.then_inc(sm["cs_ps"], 1)

                def heads(kind):
                    K = (HD, QK)[kind]
                    v = (va, vb)[kind]
                    settle()
                    with pe.Fori(0, 3) as p:
                        n = l * 48 + p * 8 + kind * 24
                        m = l * 18 + p * (2, 4)[kind] + (0, 6)[kind]
                        pe.wait_ge(sm["staged"], l * 12 + p * 2 + (6 * kind + 2))
                        for i in range(2 if kind == 0 else 4):
                            if i >= 2:
                                pe.wait_ge(sm["st_copied"], m + (i - 1))
                            for t in range(TC):
                                if kind == 0:
                                    src = (stage_qa, stage_ka)[i][:, t, :]
                                    ins = mm(ps[:, 4 + i, P * t:P * t + P], src, (flip, ident)[i], start=True, stop=True)
                                else:
                                    src = (stage_q, stage_k)[i // 2][:, t, i % 2, :]
                                    ins = tr(ps[0:QK, 4 + i % 2, P * t:P * t + P], src, ident)
                            ins.then_inc(sm["st_T"], 1)
                        pe.wait_ge(sm["st_copied"], m + (2, 4)[kind])

                        def scores(i):
                            hh, t = divmod(i, 4)
                            if kind == 0:
                                q, k = (x[HD * hh:HD * hh + HD, 0] for x in (qT, kT))
                            else:
                                q, k = (x[0:QK, hh] for x in (qT, kT))
                            mm(ps[:, i % 2, :], q[:, P * t:P * t + P], k, start=True, stop=True).then_inc(sm["s_ps"], 1)

                        scores(0)
                        for i in range(9):
                            if i < 7:
                                scores(i + 1)
                            if i < 8:
                                pe.wait_ge(sm["p_done"], n + (i + 1))
                                for k in range(TC):
                                    ins = tr(ps[:, 2 + i % 2, P * k:P * k + P], prob[:, i % 2, P * k:P * k + P], ident)
                                ins.then_inc(sm["pt_ps"], 1)
                            if i >= 1:
                                hh, t = divmod(i - 1, 4)
                                pe.wait_ge(sm["pt_copied"], n + i)
                                if i >= 3:
                                    pe.wait_ge(sm["o_done"], n + (i - 2))
                                for k in range(TC):
                                    ins = mm(ps[:, 6 + (i - 1) % 2, 0:64], probT[:, (i - 1) % 2, P * k:P * k + P],
                                             one(v[:, k:k + 1, bass.ds(p * 128 + 64 * hh, 64)]),
                                             start=(k == 0), stop=(k == TC - 1))
                                ins.then_inc(sm["o_ps"], 1)

                heads(0)
                heads(1)
                for c in range(6):
                    pe.wait_ge(sm["m_normed"], l * 2 + (1 + c // 3))
                    if c >= 2:
                        pe.wait_ge(sm["mt_copied"], l * 6 + (c - 1))
                    for t in range(TC):
                        src = mix_tok[:, t, P * c:P * c + P]
                        ins = mm(ps[:, 4 + c % 2, P * t:P * t + P], src, (flip, ident)[c // 3], start=True, stop=True)
                    ins.then_inc(sm["mt_ps"], 1)
                pe.wait_ge(sm["mt_copied"], l * 6 + 6)
                pe.wait_ge(sm["mix67"], l + 1)
                landed(4, 2)
                landed(5, 2)
                for n in range(8):
                    t, half = divmod(n, 2)
                    if n >= 4:
                        pe.wait_ge(sm["x_added"], l * 8 + (n - 3))
                    for k in range(KC):
                        w = ring2[4 + k // 4].rearrange("p (k n) -> p k n", k=4)
                        ins = mm(ps[:, n % 4, :], hnT[:, k, P * t:P * t + P], w[:, k % 4, 512 * half:512 * half + 512],
                                 start=(k == 0), stop=(k == KC - 1))
                    ins.then_inc(sm["wout_ps"], 1)
                norm2(1)
                used(4, "wout_ps", l * 8 + 8)
                used(5, "wout_ps", l * 8 + 8)
                pe.wait_ge(sm["hn_ready"], l * 16 + 16)
                for t in range(TC):
                    for k in range(KC):
                        ins = mm(ps[:, 6, EXPERTS * t:EXPERTS * t + EXPERTS], hnT[:, k, P * t:P * t + P],
                                 wr[:, bass.ds(l, 1), k, :].rearrange("p a e -> p (a e)"), start=(k == 0), stop=(k == KC - 1))
                ins.then_inc(sm["lg_ps"], 1)
                pe.wait_ge(sm["aff_done"], l + 1)
                for t in range(TC):
                    ins = tr(ps[0:EXPERTS, 7, P * t:P * t + P], lg[:, t, :], ident)
                ins.then_inc(sm["aff_ps"], 1)
                pe.wait_ge(sm["idx_done"], l + 1)
                settle()
                tr(ps[:, 6, 64:80], top_v[0:EXPERTS, :], ident[0:EXPERTS, 0:EXPERTS])
                tr(ps[:, 6, 80:96], idx_f[0:EXPERTS, 0:128], ident[0:EXPERTS, 0:EXPERTS])
                tr(ps[0:CAP, 6, 96:112], idx_f[0:EXPERTS, 128:192], ident[0:EXPERTS, 0:EXPERTS]).then_inc(sm["idx_ps"], 1)
                pe.wait_ge(sm["idx_cols"], l + 1)

                settle()
                with pe.Fori(0, EXPERTS // 2) as i:
                    for b in range(2):
                        n = l * 16 + i * 2 + b
                        pe.wait_ge(got[b], l * 128 + i * 16 + 16)
                        settle()
                        for k in range(KC):
                            ins = tr(ps[:, 5, CAP * k:CAP * k + CAP], xg[b][0:CAP, P * k:P * k + P], ident[0:CAP, 0:CAP])
                        ins.then_inc(sm["xst_ps"], 1)
                        pe.wait_ge(sm["xs_ready"], n + 1)

                        def halves(bank, lhs, s, first, last):
                            r2 = l * R2_IN[s] + i * 32 + (16 * b + R2_BASE[s])
                            pe.wait_ge(r2_in[s], r2)
                            wv = ring2[s].rearrange("p (k n) -> p k n", k=4)
                            for k in range(4):
                                for half in range(2):
                                    ins = mm(ps[CAP * half:CAP * half + CAP, bank, :], lhs(k), wv[:, k, 512 * half:512 * half + 512],
                                             start=(first and k == 0), stop=(last and k == 3))
                            return ins

                        for m, (bank, name) in enumerate(((2 * b, "g_ps"), (2 * b + 1, "u_ps"))):
                            for q in range(2):
                                ins = halves(bank, lambda k: xsT[b][:, 4 * q + k, :], 2 * m + q, q == 0, q == 1)
                                ins.then_inc(r2_used[2 * m] if q == 0 else sm[name], 1)
                        pe.wait_ge(sm["hid_done"], n + 1)
                        for c in range(4):
                            ins = tr(ps[:, 4, P * c:P * c + P], hid[b][:, P * c:P * c + P], ident)
                        ins.then_inc(sm["ht_ps"], 1)
                        pe.wait_ge(sm["ht_copied"], n + 1)
                        for q in range(2):
                            ins = halves(6 + b, lambda k: hT2[b][:, k, CAP * q:CAP * q + CAP], 4 + q, q == 0, q == 1)
                            ins.then_inc(r2_used[4] if q == 0 else sm["y2_ps"], 1)

        @block.gpsimd
        def _(pool):
            G = nc.gpsimd
            waits = Settle(pool, sm["settled"])
            chain = Chain(waits, sm["pool_step"])
            mul, add = ALU.mult, ALU.add
            cond = small[:, 13, :]
            waits.wait_ge(sm["cond"], 1)

            def mod_blocks(l, j0, pairs, done):
                with pool.Fori(0, pairs) as i:
                    n0 = chain.enter(i, 28)
                    for b in range(2):
                        n = 6 * l + j0 + b
                        col = i * (2 * D) + (j0 + b) * D

                        def load(k):
                            pool.dma_start(mod_in[k % 2], a["w_mod"][l][P * k:P * k + P, bass.ds(col, D)]) \
                                .then_inc(mod_in_s[k % 2], 16)

                        load(0)
                        load(1)
                        waits.wait_ge(sm["mod_ps"], i * 2 + (n - 1))
                        for k in range(KC):
                            waits.wait_ge(mod_in_s[k % 2], i * 128 + (64 * (done + b) + 16 * (k // 2 + 1)))
                            if k == 0:
                                chain(G.tensor_scalar(mod_acc[b], mod_in[0], cond[:, 0:1], None, mul))
                            else:
                                chain(G.tensor_scalar(mod_t, mod_in[k % 2], cond[:, k:k + 1], None, mul))
                            if k + 2 < KC:
                                load(k + 2)
                            if k > 0:
                                ins = G.tensor_tensor(mod_acc[b], mod_acc[b], mod_t, add)
                                if k < KC - 1:
                                    chain(ins)
                                else:
                                    ins.then_inc(sm["mod_sum"], 1)
                    chain.leave(n0, pairs)

            mod_blocks(0, 2, 2, 0)
            mod_blocks(1, 0, 3, 4)

            with pool.Fori(0, DEPTH) as l:
                waits.wait_ge(sm["qk_normed"], l + 1)
                for kind in range(2):
                    with pool.Fori(0, 3) as p:
                        waits.wait_ge(sm["stage_free"], l * 6 + p + (3 * kind + 1))
                        if kind == 0:
                            for i, dst in enumerate((stage_qa, stage_ka)):
                                G.tensor_copy(dst, qk[:, :, bass.ds(p * P + A_W * i, P)]).then_inc(sm["staged"], 1)
                            for i in range(2):
                                waits.wait_ge(bias_in[i], l * 96 + p * 32 + 32)
                                b = bias[i][:, :, 0:GRID]
                                mask = const[:, C_MASK:C_MASK + GRID].unsqueeze(1).to_broadcast([P, 14, GRID])
                                G.tensor_tensor(b, b, mask, add).then_inc(sm["bias_ready"], 1)
                        else:
                            for dst, x in ((stage_q, qb), (stage_k, kb)):
                                G.tensor_copy(dst, x[:, :, bass.ds(p * 2, 2), :]).then_inc(sm["staged"], 1)

                waits.wait_ge(sm["idx_cols"], l + 1)
                waits.wait_ge(sm["xn_saved"], l * 16 + 16)
                waits.wait_ge(sm["acc_saved"], l * 16 + 16)

                def gather(e, b, k):
                    G.tensor_copy(get_c[b][:, :], get_i[0:CAP, e:e + 1] if isinstance(e, int) else get_i[0:CAP, bass.ds(e, 1)]) \
                        .then_inc(sm["get_col"], 1)
                    waits.wait_ge(sm["get_col"], k)
                    G.indirect_dma_start(out=xg[b][0:CAP], out_offset=None, in_=xn_dram,
                                         in_offset=bass.IndirectOffsetOnAxis(ap=get_c[b][:, 0:1], axis=0)).then_inc(got[b], 16)

                def scatter(e, b):
                    n = l * 16 + e
                    G.tensor_copy(put_c[b][:, :], put_i[:, e:e + 1] if isinstance(e, int) else put_i[:, bass.ds(e, 1)]) \
                        .then_inc(sm["put_col"], 1)
                    waits.wait_ge(sm["put_col"], n + 1)
                    waits.wait_ge(sm["ye_done"], n + 1)
                    G.indirect_dma_start(out=out_rows, out_offset=bass.IndirectOffsetOnAxis(ap=put_c[b][:, 0:1], axis=0),
                                         in_=ye[b], in_offset=None, compute_op=add).then_inc(put[b], 16)

                def scattered(e, b):
                    waits.wait_ge(put[b], l * 128 + 16 + (e - b) * 8)
                    pool.sem_inc(sm["put_free"], 1)

                gather(0, 0, l * 16 + 1)
                gather(1, 1, l * 16 + 2)
                with pool.Fori(0, EXPERTS // 2 - 1) as i:
                    for b in range(2):
                        scatter(i * 2 + b, b)
                        waits.wait_ge(sm["xst_ps"], l * 16 + i * 2 + (b + 1))
                        gather(i * 2 + (b + 2), b, l * 16 + i * 2 + (b + 3))
                        scattered(i * 2 + b, b)
                for b in range(2):
                    scatter(EXPERTS - 2 + b, b)
                    scattered(EXPERTS - 2 + b, b)


def constants():
    import numpy as np
    c = np.zeros((P, C_N), np.float32)
    p = np.arange(P)
    c[p, C_ID + p] = 1
    c[p, C_FLIP + (p // GRID) * GRID + GRID - 1 - p % GRID] = 1
    col = GRID - 1 - p % GRID
    first = np.clip(col - 8, 0, GRID - 16)
    j = np.arange(GRID)
    c[:, C_MASK:C_MASK + GRID] = np.where((j >= first[:, None]) & (j < first[:, None] + 16), 0, -1e30)
    half = ROPE // 2
    inv = np.float32(10000.0) ** (-np.arange(half, dtype=np.float32) / np.float32(half))
    pos = (np.arange(TC)[None, :] * P + p[:, None]).astype(np.float32)
    ang = (pos[:, :, None] * inv[None, None, :]).astype(np.float32)
    c[:, C_COS:C_COS + 64] = np.cos(ang).reshape(P, 64)
    c[:, C_SIN:C_SIN + 64] = np.sin(ang).reshape(P, 64)
    for g, w in enumerate(WINDOWS):
        c[:, C_INV + 16 * g:C_INV + 16 * g + 16] = 1.0 / np.minimum(np.arange(1, 17), w)
    return c


_INS = ["x", "c", "w_mod", "b_mod", "norm_mix_g", "norm_ffn_g", "lru_w_y", "lru_b_y", "lru_w_in", "lru_b_in",
        "lru_conv_w", "lru_conv_b", "lru_w_a", "lru_b_a", "lru_w_x", "lru_b_x", "lru_lambda", "lru_w_out",
        "lru_b_out", "pool_w", "pool_scale", "ffn_w1", "ffn_w2", "final_norm_g", "norm_mix_2", "w_in_2",
        "q_norm_a_2", "k_norm_a_2", "rpb_2", "cq_norm_2", "w_uq_2", "ckv_norm_2", "w_ukv_2", "q_norm_b_2",
        "k_norm_b_2", "conv_w_2", "out_norm_2", "w_out_2", "norm_ffn_2", "w_router_2", "b_router_2",
        "w_gate_2", "w_up_2", "w_down_2"]


def kernel(**inputs):
    import numpy as np
    import concourse.bacc as bacc
    from concourse.bass_utils import run_bass_kernel_spmd as run

    nc = bacc.Bacc("TRN2", target_bir_lowering=False, num_devices=1)
    arrays, aps = {}, {}
    for name in _INS:
        arr = np.ascontiguousarray(inputs[name])
        arrays[f"in_{name}"] = arr
        aps[name] = nc.dram_tensor(f"in_{name}", arr.shape, mybir.dt.from_np(arr.dtype), kind="ExternalInput").ap()
    arrays["consts"] = constants()
    aps["consts"] = nc.dram_tensor("consts", (P, C_N), F32, kind="ExternalInput").ap()
    out = nc.dram_tensor("out", (1, S, D), F32, kind="ExternalOutput").ap()
    program(nc, aps, out)
    r = run(nc, [arrays], core_ids=[0])
    return r.results[0]["out"]
```

```python
from contextlib import ExitStack

import concourse.bass as bass
from concourse import mybir

F32 = mybir.dt.float32
U32 = mybir.dt.uint32
ACT = mybir.ActivationFunctionType
ALU = mybir.AluOpType
AX = mybir.AxisListType

P = 128
D = 1024
S = 512
KC = D // P
TC = S // P
FF = 4096
FC = FF // P
DEPTH = 2
EPS = 1e-6
WINDOWS = (2, 4, 8, 16)
PAD = 16
GRID = 64
NA_HEADS, HD = 6, 64
A_W = NA_HEADS * HD
RPB_H, RPB_W = 15, 31
TOEP = 2 * GRID - 1
B_HEADS, QK, NOPE, ROPE, VD = 6, 96, 64, 32, 64
QR, KVR = 256, 128
CONV = 256
EXPERTS, CAP, EFF = 16, 64, 1024
SLOT = 4096
GELU_C = 0.7978845608028654
VROWS = 35
DVE_LAYER = 173

ROW_A = dict(norm_mix_g=0, norm_ffn_g=16, lru_b_y=32, lru_b_in=40, lru_conv_w=48, lru_conv_b=80,
             lru_b_a=88, lru_b_x=96, lru_lambda=104, lru_b_out=112, pool_scale=120)
B_MOD, B_FINAL, B_C, B_ROWS = 0, 96, 104, 112
G_MIX, G_FFN, G_OUT, G_CQ, G_CKV, G_CONV, G_QA, G_KA = 0, 8, 16, 24, 26, 27, 33, 34

C_ID, C_FLIP, C_MASK, C_COS, C_SIN, C_INV, C_N = 0, 128, 256, 320, 384, 448, 512


class Chain:

    def __init__(self, eng, sem):
        self.eng, self.sem, self.n, self.loops = eng, sem, 0, []

    def value(self):
        v = self.n
        for reg, per in self.loops:
            v = reg * per + v
        return v

    def __call__(self, ins):
        self.n += 1
        ins.then_inc(self.sem, 1)
        self.eng.wait_ge(self.sem, self.value())

    def enter(self, reg, per):
        self.loops.append((reg, per))
        return self.n

    def leave(self, n0, count):
        reg, per = self.loops.pop()
        assert self.n - n0 == per, (self.n - n0, per)
        self.n = n0 + per * count


class Settle:

    def __init__(self, eng, sem):
        self.eng, self.sem = eng, sem

    def __call__(self):
        self.eng.sem_inc(self.sem, 1)

    def wait_ge(self, sem, value):
        self.eng.wait_ge(sem, value)
        if not isinstance(value, int):
            self()


def R1_IN(s, f):
    if s:
        return 16 * (f + 1)
    return 16 * (f + 1) + (112 if f >= 2 else 0) + (48 if f >= 7 else 0)


def one(ap):
    return ap.rearrange("p a n -> p (a n)")


def program(nc, a, out):
    with ExitStack() as ctx:
        def sb(name, shape, dt=F32):
            return ctx.enter_context(nc.sbuf_tensor(name, shape, dt))

        def sem(name):
            return ctx.enter_context(nc.semaphore(name))

        arena = sb("arena", [P, 50176])

        def at(lo, n, pat=None, **kw):
            v = arena[:, lo:lo + n]
            return v.rearrange(pat, **kw) if pat else v

        ps = ctx.enter_context(nc.psum_tensor("ps", [P, 8, 512], F32))
        const = sb("const", [P, C_N])
        ident, flip = const[:, C_ID:C_ID + P], const[:, C_FLIP:C_FLIP + P]
        ones = sb("ones", [P, P])
        vrow = sb("vrow", [P, 3, P])
        vA = sb("vA", [P, P])
        vB = sb("vB", [P, B_ROWS])
        v2 = sb("v2", [P, DEPTH * VROWS])
        modc = sb("modc", [P, 96])
        small = sb("small", [P, 16, 8])
        qkg = sb("qkg", [P, 2, DEPTH, QK])
        wr = sb("wr", [P, DEPTH, KC, EXPERTS])
        br = sb("br", [P, DEPTH, EXPERTS])
        ring1 = [at(SLOT * s, SLOT) for s in range(4)]
        big = 16384
        gelu_b = at(big, 4096, "p (k n) -> p k n", k=KC)
        xr = at(big + 4096, KC * 515, "p (k n) -> p k n", k=KC)
        xc = at(big + 4096 + 4120, 4096, "p (k n) -> p k n", k=KC)
        u2 = at(big, 16384, "p (k n) -> p k n", k=FC)
        x_rows = at(big, 4096, "p (t d) -> p t d", t=TC)
        hp = at(big, KC * (PAD + S), "p (k n) -> p k n", k=KC)
        pw = [at(big + 4224 + 1056 * i, 1056, "p (k n) -> p k n", k=2) for i in range(2)]
        acc0 = [at(big + 4096 + 1024 * i, 1024) for i in range(2)]
        gate_v = at(big + 4096 + 4120 + 4096, 4096, "p (k n) -> p k n", k=KC)
        xT = at(32800, 4096, "p (k n) -> p k n", k=KC)
        hT = at(36896, 4096, "p (k n) -> p k n", k=KC)
        squares = [hT if u % 2 == 0 else at(big + 12288, 4096, "p (k n) -> p k n", k=KC) for u in range(5)]
        mod_in = [at(40992 + 1024 * i, 1024) for i in range(2)]
        mod_acc = [at(43040 + 1024 * i, 1024) for i in range(2)]
        mod_t = at(45088, 1024)
        tmp = [at(46112 + 512 * i, 512) for i in range(6)]
        ring2 = [at(SLOT * s, SLOT) for s in range(8)]
        x_tok = at(24576, 4096, "p (t d) -> p t d", t=TC)
        hnT = at(28672, 4096, "p (k n) -> p k n", k=KC)
        R = 32768
        xn = at(R, 4096, "p (t d) -> p t d", t=TC)
        qk = at(R, 3072, "p (t d) -> p t d", t=TC)
        va = at(R + 3072, 1536, "p (t d) -> p t d", t=TC)
        qb = at(R + 4608, 2304, "p (t h d) -> p t h d", t=TC, h=B_HEADS)
        kb = at(R + 6912, 2304, "p (t h d) -> p t h d", t=TC, h=B_HEADS)
        vb = at(R + 9216, 1536, "p (t d) -> p t d", t=TC)
        oc = at(R + 10752, 1024, "p (k n) -> p k n", k=2)
        W = R + 11776
        cv = at(W, 3072, "p (k n) -> p k n", k=6)
        cu = at(W + 3072, 1028, "p (k n) -> p k n", k=2)
        cvs = at(W + 4100, 1024, "p (k n) -> p k n", k=2)
        p3 = at(W, 1664, "p (t d) -> p t d", t=TC)
        p3sq = at(W + 1664, 1536, "p (t d) -> p t d", t=TC)
        cT = at(W + 3200, 1536, "p (k n) -> p k n", k=3)
        normsq = ring2[3][:, 0:3072]
        ropet = [ring2[3][:, 384 * i:384 * i + 384].rearrange( "p (t h d) -> p t h d", t=TC, h=B_HEADS) for i in range(4)]
        bias = [ring2[3][:, 1778 * i:1778 * i + 1778].rearrange("p (r n) -> p r n", r=14) for i in range(2)]
        stage_q = at(W, 768, "p (t h d) -> p t h d", t=TC, h=2)
        stage_k = at(W + 768, 768, "p (t h d) -> p t h d", t=TC, h=2)
        stage_qa = at(W, 512, "p (t d) -> p t d", t=TC)
        stage_ka = at(W + 768, 512, "p (t d) -> p t d", t=TC)
        qT = at(W + 1536, 1024, "p (h n) -> p h n", h=2)
        kT = at(W + 2560, 1024, "p (h n) -> p h n", h=2)
        prob = at(W + 3584, 1024, "p (b n) -> p b n", b=2)
        probT = at(W + 4608, 1024, "p (b n) -> p b n", b=2)
        mix_sq = at(W, 1536, "p (t h d) -> p t h d", t=TC, h=6)
        mix_tok = at(W + 1536, 3072, "p (t c) -> p t c", t=TC)
        wr_l = at(W, KC * EXPERTS, "p (k e) -> p k e", k=KC)
        lg_T = at(W + 128, 512)
        lg = at(R + 4096, 64, "p (t e) -> p t e", t=TC)
        st = sb("st", [P, 160])
        aff = at(R + 4160, 512)
        aff2 = at(R + 4672, 512)
        top_v = at(R + 5184, 128)
        top_i = at(R + 5312, 64).bitcast(U32)
        idx_f = at(R + 5376, 192)
        gate_t = at(R + 5568, 16)
        put_i = at(R + 5584, 16).bitcast(U32)
        get_i = at(R + 5600, 16).bitcast(U32)
        get_c = [sb(f"get_c{i}", [CAP, 1], U32) for i in range(2)]
        put_c = [sb(f"put_c{i}", [P, 1], U32) for i in range(2)]
        xg = [at(R + 5632 + 1024 * i, 1024) for i in range(2)]
        xsT = [at(R + 7680 + 512 * i, 512, "p (k n) -> p k n", k=KC) for i in range(2)]
        hid = [at(R + 8704 + 512 * i, 512) for i in range(2)]
        hidt = [at(R + 9728 + 512 * i, 512) for i in range(2)]
        hT2 = [at(R + 10752 + 512 * i, 512, "p (k n) -> p k n", k=4) for i in range(2)]
        ye = [at(R + 11776 + 512 * i, 512) for i in range(2)]
        toep = nc.dram_tensor("toep", (DEPTH, NA_HEADS * RPB_H * TOEP), F32, kind="Internal").ap()
        xn_dram = nc.dram_tensor("xn_rows", (S, D), F32, kind="Internal").ap()
        toep_sb = at(46112 + 3072, 2 * TOEP + 2, "p (l n) -> p l n", l=2)
        out_t = out.rearrange("b (t p) d -> p (b t) d", p=P)
        out_rows = out.rearrange("b t (h d) -> (b t h) d", h=2)

        names = """const_in vecB_in vecA_in vec2_in x_in toep_zero rpb_in toep_out
          vec_T vec_cols xr_T x_done cond_t cond mod_sum mod_ps mod_cols
          sq_done ss_done inv_done rstd_done hn_part h_done
          lam lru_const
          y_ps y_sb y_sq y_arg y_tanh xi_ps xi_sb conv_done
          gate_ps gate_act gate_free neg_done sqrt_done z_done wo_ps
          f1_ps relu_done u_free f2_ps pool_done wp_ps fin_done fin_T x_ready
          n_ss n_inv n_rstd xn_done xt_ps hn_ready gains_in
          proj_ps proj_copied conv_ps conv_copied conv_sq cs_ps c_inv c_rstd conv_out
          c_ss c_r c_normed ct_ps ct_copied p2_ps p2_copied qk_ss qk_r qk_normed
          staged st_T st_copied bias_ready bias_used s_ps s_max p_done pt_ps pt_copied o_ps o_done
          m_ss m_r m_normed mt_ps mt_copied wout_ps x_added acc_saved xn_saved
          lg_ps lg_max lg_exp aff_done aff_ps idx_done idx_ps idx_cols
          xst_ps xs_ready g_ps g_tanh u_ps hid_done ht_ps ht_copied y2_ps ye_done
          dve_step pool_step gain_done settled get_col put_col fin_copied stage_free put_free gains_set kr_copied lt_sb""".split()
        sm = {n: sem(n) for n in names}
        r1_in = [sem(f"ring1_in{s}") for s in range(4)]
        r1_used = [sem(f"ring1_used{s}") for s in range(4)]
        r2_in = [sem(f"ring2_in{s}") for s in range(8)]
        r2_used = [sem(f"ring2_used{s}") for s in range(6)]
        mod_in_s = [sem(f"mod_in{i}") for i in range(2)]
        bias_in = [sem(f"bias_in{i}") for i in range(2)]
        got = [sem(f"rows_got{i}") for i in range(2)]
        put = [sem(f"rows_put{i}") for i in range(2)]
        F_FFN = ([3, 3, 3, 2], [8, 7, 7, 6])
        O_FFN = (0, 1)
        R1_FILLS = (12, 11, 11, 10)
        USES = [9, 9, 17, 17, 18, 18]

        R2_IN = [160, 160, 288, 272, 288, 288, 128, 128]
        R2_BASE = [48, 48, 48, 32, 48, 48, 16, 16]

        block = ctx.enter_context(nc.Block())

        @block.sync
        def _(sp):
            sp.dma_start(const[:, :], a["consts"]).then_inc(sm["const_in"], 16)
            sp.wait_ge(sm["vecB_in"], 48)
            fills = [0, 0, 0, 0]
            settle = Settle(sp, sm["settled"])

            def fill(s, dst, src):
                if fills[s] >= 1:
                    sp.wait_ge(r1_used[s], fills[s])
                fills[s] += 1
                sp.dma_start(dst, src).then_inc(r1_in[s], 16)

            def k_rows(w, c0, c1, k0=0, k1=KC):
                return w.rearrange("(k p) n -> p k n", p=P)[:, k0:k1, c0:c1]

            def slot(s, k):
                return ring1[s].rearrange("p (k n) -> p k n", k=k)

            for m in range(4):
                j, half = divmod(m, 2)
                if m == 2:
                    sp.dma_start(x_rows, a["x"].rearrange("b (t p) d -> p (b t) d", p=P)).then_inc(sm["x_in"], 16)
                fill(m, slot(m, 4), k_rows(a["w_mod"][0], j * D, (j + 1) * D, 4 * half, 4 * half + 4))
            for i in range(2):
                fill(i, slot(i, KC), k_rows(a["lru_w_y"][0], 512 * i, 512 * i + 512))
            for i in range(2):
                fill(2 + i, slot(2 + i, KC), k_rows(a["lru_w_in"][0], 512 * i, 512 * i + 512))
            for n, w in enumerate(("lru_w_a", "lru_w_x")):
                if n == 0:
                    sp.wait_ge(r1_used[0], fills[0])
                    fills[0] += 1
                for h in range(4):
                    sp.dma_start(ring1[0][:, n * 2048 + h * 512:n * 2048 + h * 512 + 512]
                                 .rearrange("p (i n) -> p i n", i=2),
                                 a[w][0, h].rearrange("(i p) n -> p i n", p=P)).then_inc(r1_in[0], 16)
            for i in range(2):
                fill(1 + i, slot(1 + i, KC), k_rows(a["lru_w_out"][0], 512 * i, 512 * i + 512))

            def ffn(l):
                f0, o = F_FFN[l], O_FFN[l]
                settle()
                with sp.Fori(0, 2) as i:
                    for b in range(4):
                        s = (o + b) % 4
                        sp.wait_ge(r1_used[s], i + f0[s])
                        sp.dma_start(slot(s, KC), a["ffn_w1"][l].rearrange("(k p) n -> p k n", p=P)
                                     [:, :, bass.ds(i * 2048 + 512 * b, 512)]).then_inc(r1_in[s], 16)
                settle()
                with sp.Fori(0, 2) as i:
                    for b in range(4):
                        s = (o + b) % 4
                        sp.wait_ge(r1_used[s], i + (f0[s] + 2))
                        sp.dma_start(slot(s, FC), a["ffn_w2"][l].rearrange("(k p) n -> p k n", p=P)
                                     [:, :, bass.ds(i * 512 + P * b, P)]).then_inc(r1_in[s], 16)

            ffn(0)
            sp.wait_ge(r1_used[0], 7)
            for g in range(4):
                sp.dma_start(ring1[0][:, g * 512:g * 512 + 512].rearrange("p (i n) -> p i n", i=2),
                             a["pool_w"][0, g].rearrange("(i p) n -> p i n", p=P)).then_inc(r1_in[0], 16)
            ffn(1)

            for s in range(4):
                sp.wait_ge(r1_used[s], R1_FILLS[s])
            sp.wait_ge(sm["x_done"], 40)
            with sp.Fori(0, DEPTH) as l:
                w_in = a["w_in_2"][bass.ds(l, 1)].rearrange("a (k p) n -> p (a k) n", p=P)
                uq = a["w_uq_2"][bass.ds(l, 1)].rearrange("a (k p) n -> p (a k) n", p=P)
                edge = [0, 384, 768, 1152, 1568, 1952, 2336]
                for s in range(6):
                    n = edge[s + 1] - edge[s]
                    sp.wait_ge(r2_used[s], l * USES[s] + 1)
                    sp.dma_start(ring2[s][:, 0:KC * n].rearrange("p (k n) -> p k n", k=KC),
                                 w_in[:, :, edge[s]:edge[s + 1]]).then_inc(r2_in[s], 16)
                    if s == 0:
                        sp.dma_start(ring2[0][:, 3072:3840],
                                     a["w_ukv_2"][bass.ds(l, 1)].rearrange("a p n -> (a p) n")).then_inc(r2_in[0], 16)
                    elif s < 3:
                        sp.dma_start(ring2[s][:, 3072:3648], uq[:, s - 1, :]).then_inc(r2_in[s], 16)
                    if s == 0:
                        sp.wait_ge(sm["x_ready"], l * 16 + 16)
                w_out = a["w_out_2"][bass.ds(l, 1)].rearrange("a (k p) n -> p (a k) n", p=P)
                def bias_tiles(h, i):
                    src = toep[bass.ds(l, 1), bass.ds(h * (RPB_H * TOEP), RPB_H * TOEP)]
                    for q in range(2):
                        view = bass.AP(src.tensor, src.offset + (1 - q) * TOEP, [[1, GRID], [1, 13 * TOEP + GRID]])
                        sp.dma_start(bias[i][q * GRID:(q + 1) * GRID].rearrange("p r n -> p (r n)")
                                     [:, 0:13 * TOEP + GRID], view).then_inc(bias_in[i], 16)

                sp.wait_ge(sm["toep_out"], 32)
                sp.wait_ge(sm["qk_normed"], l + 1)
                for i in range(2):
                    bias_tiles(i, i)
                for s in (4, 5):
                    sp.wait_ge(r2_used[s], l * USES[s] + 2)
                    sp.dma_start(ring2[s].rearrange("p (k n) -> p k n", k=4),
                                 w_out[:, 4 * (s - 4):4 * (s - 4) + 4, :]).then_inc(r2_in[s], 16)
                settle()
                with sp.Fori(0, 2) as p:
                    for i in range(2):
                        sp.wait_ge(sm["bias_used"], l * 6 + p * 2 + (i + 1))
                        bias_tiles(p * 2 + (i + 2), i)

                settle()
                def expert_half(e, de, n, w):
                    we = a[w][bass.ds(l, 1), bass.ds(e + de, 1)].rearrange("a b (k p) n -> p (a b k) n", p=P)
                    for i in range(2):
                        s = 6 + i if n == 0 and de % 2 else 2 * n + i
                        if s < 2:
                            sp.wait_ge(r2_used[s], l * USES[s] + half(e) + (de // 2 + 2))
                        elif s < 6:
                            sp.wait_ge(r2_used[s], l * USES[s] + e + (de + (2 if s < 4 else 3)))
                        elif i == 0 and de == 1 and isinstance(e, int):
                            sp.wait_ge(sm["acc_saved"], l * 16 + 16)
                        elif de == 1 and isinstance(e, int):
                            sp.wait_ge(sm["lg_ps"], l * 2 + 1)
                        else:
                            sp.wait_ge(sm["g_ps"], l * 16 + e + (de - 1))
                        sp.dma_start(ring2[s].rearrange("p (k n) -> p k n", k=4),
                                     we[:, 4 * i:4 * i + 4, :]).then_inc(r2_in[s], 16)

                gate, up, down = ((0, "w_gate_2"), (1, "w_up_2"), (2, "w_down_2"))

                def half(e):
                    return e // 2 if isinstance(e, int) else pair_i

                for de, w in ((0, gate), (0, up), (0, down), (1, gate)):
                    expert_half(0, de, *w)
                with sp.Fori(0, EXPERTS // 2 - 1) as pair_i:
                    for b in range(2):
                        for de, w in ((b + 2, gate), (b + 1, up), (b + 1, down)):
                            expert_half(pair_i * 2, de, *w)
                for w in (up, down):
                    expert_half(EXPERTS - 2, 1, *w)

        @block.scalar
        def _(act):
            settle = Settle(act, sm["settled"])

            def A(out, in_, *args, **kw):
                if settling:
                    settle()
                return nc.scalar.activation(out, in_, *args, **kw)

            settling = []
            act.sem_inc(sm["u_free"], 4)
            act.sem_inc(sm["gate_free"], 2)
            act.sem_inc(sm["put_free"], 2)
            act.sem_inc(sm["stage_free"], 1)
            for s in range(6):
                act.sem_inc(r2_used[s], 1)
            act.dma_start(vrow[104:112, 1, :], a["c"].rearrange("a (r p) -> (a r) p", p=P)).then_inc(sm["vecB_in"], 16)
            act.dma_start(vrow[0:96, 1, :], a["b_mod"].rearrange("a (r p) -> (a r) p", p=P)).then_inc(sm["vecB_in"], 16)
            act.dma_start(vrow[96:104, 1, :], a["final_norm_g"].rearrange("(r p) -> r p", p=P)).then_inc(sm["vecB_in"], 16)
            for n, r in ROW_A.items():
                v = a[n]
                v = v.rearrange("a (r p) -> (a r) p", p=P) if len(v.shape) == 2 else \
                    v.rearrange("a b (r p) -> (a b r) p", p=P)
                act.dma_start(vrow[r:r + v.shape[0], 0, :], v).then_inc(sm["vecA_in"], 16)

            def second_vectors(l):
                o = l * VROWS
                for n, r, k in (("norm_mix_2", G_MIX, 8), ("norm_ffn_2", G_FFN, 8), ("out_norm_2", G_OUT, 8),
                                ("cq_norm_2", G_CQ, 2), ("ckv_norm_2", G_CKV, 1)):
                    act.dma_start(vrow[o + r:o + r + k, 2, :],
                                  a[n][l].rearrange("(r p) -> r p", p=P)).then_inc(sm["vec2_in"], 16)
                act.dma_start(vrow[o + G_CONV:o + G_CONV + 6, 2, :],
                              a["conv_w_2"][l].rearrange("w (r p) -> (w r) p", p=P)).then_inc(sm["vec2_in"], 16)
                for n, r in (("q_norm_a_2", G_QA), ("k_norm_a_2", G_KA)):
                    for i in range(2):
                        act.dma_start(vrow[o + r:o + r + 1, 2, HD * i:HD * i + HD],
                                      a[n][l:l + 1, :]).then_inc(sm["vec2_in"], 16)

            act.wait_ge(sm["vec_cols"], 1)
            A(small[:, 0, :], vB[:, B_C:B_C + 8], ACT.Tanh, scale=0.5).then_inc(sm["cond_t"], 1)
            for k in range(KC):
                act.wait_ge(sm["xr_T"], k + 1)
                A(xT[:, k, :], ps[:, k % 4, :], ACT.Copy).then_inc(sm["x_done"], 1)
            act.wait_ge(sm["vec_T"], 2)
            A(vA[:, :], ps[:, 4, 0:P], ACT.Copy).then_inc(sm["vec_cols"], 1)
            act.wait_ge(sm["vec_cols"], 2)
            A(small[:, 1, :], vA[:, 104:112], ACT.Abs).then_inc(sm["lam"], 1)
            act.wait_ge(sm["lam"], 1)
            A(small[:, 2, :], small[:, 1, :], ACT.Exp, scale=-1.0).then_inc(sm["lam"], 1)
            A(small[:, 3, :], vA[:, 88:96], ACT.Copy, scale=0.5).then_inc(sm["lru_const"], 1)
            A(small[:, 4, :], vA[:, 96:104], ACT.Copy, scale=0.5).then_inc(sm["lru_const"], 1)

            def second_tables():
                for l in range(DEPTH):
                    second_vectors(l)
                    act.dma_start(wr[:, l, :, :], a["w_router_2"][l].rearrange("(k p) e -> p k e", p=P)).then_inc(sm["gains_in"], 16)
                    act.dma_start(br[:, l, :], a["b_router_2"][l:l + 1, :].partition_broadcast(P)).then_inc(sm["gains_in"], 16)
                    for i, n in enumerate(("q_norm_b_2", "k_norm_b_2")):
                        act.dma_start(qkg[:, i, l, :], a[n][l:l + 1, :].partition_broadcast(P)).then_inc(sm["gains_in"], 16)
                act.wait_ge(sm["toep_zero"], 1)
                for l in range(DEPTH):
                    act.dma_start(toep_sb[0:90, l, GRID - RPB_W // 2 - 1:GRID - RPB_W // 2 - 1 + RPB_W],
                                  a["rpb_2"][l].rearrange("h r c -> (h r) c")).then_inc(sm["rpb_in"], 16)
                act.wait_ge(sm["rpb_in"], 32)
                for l in range(DEPTH):
                    act.dma_start(toep[l].rearrange("(r c) -> r c", c=TOEP), toep_sb[0:90, l, 0:TOEP]).then_inc(sm["toep_out"], 16)

            def norm(u):
                for k in range(KC):
                    act.wait_ge(sm["x_done"], 8 * u + k + 1)
                    A(squares[u][:, k, :], xT[:, k, :], ACT.Square).then_inc(sm["sq_done"], 1)
                act.wait_ge(sm["inv_done"], u + 1)
                A(tmp[1], tmp[0], ACT.Sqrt).then_inc(sm["rstd_done"], 1)
                if u == 4:
                    return
                l, g, sh = u // 2, 5 + u, (0, 3)[u % 2]
                for k in range(KC):
                    act.wait_ge(sm["hn_part"], 8 * u + k + 1)
                    dst = hp[:, k, PAD:] if u == 2 else hT[:, k, :]
                    A(dst, hT[:, k, :], ACT.Identity, scale=small[:, g, k:k + 1],
                      bias=modc[:, l * 48 + sh * 8 + k:l * 48 + sh * 8 + k + 1]).then_inc(sm["h_done"], 1)

            norm(0)
            second_tables()

            settling.append(1)
            with act.Fori(0, 2) as i:
                for b in range(4):
                    c, t = i * 4 + b, tmp[2 + b % 2]
                    act.wait_ge(sm["y_ps"], c + 1)
                    A(one(gelu_b[:, bass.ds(c, 1), :]), ps[:, b, :], ACT.Identity,
                      bias=vA[:, bass.ds(c + 32, 1)]).then_inc(sm["y_sb"], 1)
                    act.wait_ge(sm["y_sb"], c + 1)
                    A(t, one(gelu_b[:, bass.ds(c, 1), :]), ACT.Square).then_inc(sm["y_sq"], 1)
                    act.wait_ge(sm["y_arg"], c + 1)
                    A(t, t, ACT.Tanh, scale=GELU_C).then_inc(sm["y_tanh"], 1)
            for s in range(2):
                act.sem_inc(r1_used[s], 1)

            def x_in(c, b):
                act.wait_ge(sm["xi_ps"], c + 1)
                A(one(xr[:, bass.ds(c, 1), 3:515]), ps[:, b, :], ACT.Identity,
                  bias=vA[:, bass.ds(c + 40, 1)]).then_inc(sm["xi_sb"], 1)

            def gates(c, j):
                t, n0 = tmp[2 + j], c * 3
                act.wait_ge(sm["gate_ps"], c + 1)
                A(t, ps[:, 2 + 2 * j, :], ACT.Tanh, scale=0.5, bias=small[:, 3, bass.ds(c, 1)]).then_inc(sm["gate_act"], 1)
                act.wait_ge(sm["gate_act"], n0 + 1)
                A(one(xr[:, bass.ds(c, 1), 0:512]), t, ACT.Tanh, scale=small[:, 10, bass.ds(c, 1)],
                  bias=small[:, 10, bass.ds(c, 1)]).then_inc(sm["gate_act"], 1)
                act.wait_ge(sm["gate_free"], c + 1)
                A(tmp[4 + j], ps[:, 3 + 2 * j, :], ACT.Tanh, scale=0.5, bias=small[:, 4, bass.ds(c, 1)]).then_inc(sm["gate_act"], 1)

            act.wait_ge(sm["lru_const"], 3)
            for j in range(2):
                x_in(j, j)
            with act.Fori(0, 3) as h:
                for j in range(2):
                    x_in(h * 2 + (2 + j), j)
                for j in range(2):
                    gates(h * 2 + j, j)
            for s in (2, 3):
                act.sem_inc(r1_used[s], 1)
            for j in range(2):
                gates(6 + j, j)
            act.sem_inc(r1_used[0], 1)
            with act.Fori(0, KC) as c:
                act.wait_ge(sm["neg_done"], c + 1)
                A(one(xr[:, bass.ds(c, 1), 0:512]), one(xr[:, bass.ds(c, 1), 0:512]), ACT.Sqrt).then_inc(sm["sqrt_done"], 1)

            settling.clear()

            def ffn(l):
                with act.Fori(0, 2) as i:
                    for b, j in ((b, j) for b in range(4) for j in range(4)):
                        c = i * 16 + (4 * b + j)
                        act.wait_ge(sm["f1_ps"], c + (l * 32 + 1))
                        if j == 3:
                            act.sem_inc(r1_used[(O_FFN[l] + b) % 4], 1)
                        act.wait_ge(sm["u_free"], c + (l * 32 + 3))
                        A(tmp[2 + j % 2], ps[:, j, :], ACT.Relu).then_inc(sm["relu_done"], 1)

            norm(1)
            ffn(0)
            norm(2)
            norm(3)
            ffn(1)
            norm(4)

            act.wait_ge(sm["toep_out"], 32)
            with act.Fori(0, DEPTH) as l:
                act.wait_ge(sm["x_ready"], l * 16 + 16)
                gain = st[:, 96:96 + VROWS]
                A(gain, v2[:, bass.ds(l * VROWS, VROWS)], ACT.Copy).then_inc(sm["gains_set"], 1)
                act.wait_ge(sm["gains_set"], l + 1)

                def norm2(w):
                    for t in range(TC):
                        if w == 1:
                            act.wait_ge(sm["x_added"], l * 8 + (2 * t + 2))
                        A(xn[:, t, :], x_tok[:, t, :], ACT.Square, accum_out=st[:, t:t + 1]).then_inc(sm["n_ss"], 1)
                    act.wait_ge(sm["n_inv"], l * 2 + (w + 1))
                    A(st[:, 8:12], st[:, 4:8], ACT.Sqrt).then_inc(sm["n_rstd"], 1)
                    for k in range(KC):
                        act.wait_ge(sm["xt_ps"], l * 16 + (8 * w + k + 1))
                        A(hnT[:, k, :], ps[:, 4 + k % 2, :], ACT.Copy,
                          scale=gain[:, (G_MIX, G_FFN)[w] + k:(G_MIX, G_FFN)[w] + k + 1]).then_inc(sm["hn_ready"], 1)

                norm2(0)
                for j, dst in enumerate((qk[:, :, 0:384], qk[:, :, 384:768], va, p3)):
                    for t in range(TC):
                        act.wait_ge(sm["proj_ps"], l * 16 + (4 * j + t + 1))
                        n = dst.shape[2]
                        A(dst[:, t, :], ps[:, t, 0:n], ACT.Copy).then_inc(sm["proj_copied"], 1)

                def head_root(i):
                    act.wait_ge(sm["qk_ss"], l * 2 + (i + 1))
                    A(st[:, 48:96], st[:, 48:96], ACT.Sqrt).then_inc(sm["qk_r"], 1)

                act.wait_ge(sm["c_ss"], l + 1)
                A(st[:, 24:32], st[:, 16:24], ACT.Sqrt).then_inc(sm["c_r"], 1)
                for i in range(3):
                    act.wait_ge(sm["ct_ps"], l * 3 + (i + 1))
                    A(cT[:, i, :], ps[:, 4 + i, :], ACT.Copy, scale=gain[:, G_CQ + i:G_CQ + i + 1]).then_inc(sm["ct_copied"], 1)
                for t in range(TC):
                    if t == 2:
                        head_root(0)
                    for i in range(2):
                        act.wait_ge(sm["p2_ps"], l * 16 + (4 * t + i + 1))
                        A(qb[:, t, 3 * i:3 * i + 3, :], ps[:, i, 0:288].rearrange("p (h d) -> p h d", h=3), ACT.Copy) \
                            .then_inc(sm["p2_copied"], 1)
                    for i in range(2):
                        act.wait_ge(sm["p2_ps"], l * 16 + (4 * t + i + 3))
                        kv = ps[:, 2 + i, 0:384].rearrange("p (h d) -> p h d", h=3)
                        A(kb[:, t, 3 * i:3 * i + 3, 0:NOPE], kv[:, :, 0:NOPE], ACT.Copy)
                        A(vb[:, t, 192 * i:192 * i + 192].rearrange("p (h d) -> p h d", h=3), kv[:, :, NOPE:], ACT.Copy) \
                            .then_inc(sm["p2_copied"], 1)
                act.wait_ge(sm["p2_ps"], l * 16 + 16)
                act.wait_ge(sm["kr_copied"], l + 1)
                for c in range(6):
                    act.wait_ge(sm["conv_ps"], l * 6 + (c + 1))
                    A(cv[:, (0, 4, 2, 1, 5, 3)[c], :], ps[:, 4 + c % 4, :], ACT.Copy).then_inc(sm["conv_copied"], 1)
                    if c == 1:
                        head_root(1)
                act.wait_ge(sm["c_inv"], l + 1)
                A(cvs[:, 1, :], cvs[:, 0, :], ACT.Sqrt).then_inc(sm["c_rstd"], 1)

                def stage(kind, p, dp, steps):
                    for i in steps:
                        act.wait_ge(sm["st_T"], l * 18 + p * (2, 4)[kind] + ((0, 6)[kind] + (2, 4)[kind] * dp + i + 1))
                        if kind == 0:
                            for rows, h in ((slice(0, P), 0),) if i == 0 else ((slice(0, HD), 0), (slice(HD, P), 1)):
                                ins = A((qT, kT)[i][rows, h, :], ps[rows, 4 + i, :], ACT.Copy,
                                        scale=gain[rows, G_QA + i:G_QA + i + 1])
                            ins.then_inc(sm["st_copied"], 1)
                        else:
                            A((qT, kT)[i // 2][0:QK, i % 2, :], ps[0:QK, 4 + i % 2, :], ACT.Copy).then_inc(sm["st_copied"], 1)
                    if steps[-1] == (1, 3)[kind]:
                        act.sem_inc(sm["stage_free"], 1)

                def pair(kind, p, following):
                    n = l * 48 + p * 8 + kind * 24
                    for i in range(9):
                        if i < 8:
                            act.wait_ge(sm["s_max"], n + (i + 1))
                            src = prob[:, i % 2, :] if kind == 0 else ps[:, i % 2, :]
                            A(prob[:, i % 2, :], src, ACT.Exp, bias=st[:, 32 + i:33 + i],
                              scale=(1.0, QK ** -0.5)[kind], accum_out=st[:, 40 + i:41 + i]).then_inc(sm["p_done"], 1)
                        if i >= 1:
                            act.wait_ge(sm["pt_ps"], n + i)
                            if i >= 3:
                                act.wait_ge(sm["o_ps"], n + (i - 2))
                            A(probT[:, (i - 1) % 2, :], ps[:, 2 + (i - 1) % 2, :], ACT.Copy).then_inc(sm["pt_copied"], 1)
                        if i == 7 and following:
                            stage(*following, range(2))
                        if i == 8 and following and following[0] == 1:
                            stage(*following, range(2, 4))

                stage(0, 0, 0, range(2))
                for kind in range(2):
                    with act.Fori(0, 2) as p:
                        pair(kind, p, (kind, p, 1))
                    pair(kind, 2, (1, 0, 0) if kind == 0 else None)
                act.wait_ge(sm["m_ss"], l + 1)
                A(st[:, 16:24], st[:, 16:24], ACT.Sqrt).then_inc(sm["m_r"], 1)
                for c in range(6):
                    act.wait_ge(sm["mt_ps"], l * 6 + (c + 1))
                    A(hnT[:, c, :], ps[:, 4 + c % 2, :], ACT.Copy, scale=gain[:, G_OUT + c:G_OUT + c + 1]).then_inc(sm["mt_copied"], 1)
                norm2(1)
                act.dma_start(out_t, x_tok).then_inc(sm["acc_saved"], 16)
                act.wait_ge(sm["xn_done"], l * 8 + 8)
                act.dma_start(xn_dram.rearrange("(t p) d -> p t d", p=P), xn).then_inc(sm["xn_saved"], 16)
                act.wait_ge(sm["lg_max"], l + 1)
                A(lg.rearrange("p t e -> p (t e)"), lg.rearrange("p t e -> p (t e)"), ACT.Exp).then_inc(sm["lg_exp"], 1)
                with act.Fori(0, EXPERTS // 2) as i:
                    for b in range(2):
                        n = l * 16 + i * 2 + b
                        act.wait_ge(sm["g_ps"], n + 1)
                        if b == 0:
                            act.sem_inc(r2_used[1], 1)
                        A(hidt[b], ps[:, 2 * b, :], ACT.Tanh, scale=0.5).then_inc(sm["g_tanh"], 1)
                        act.wait_ge(sm["ht_ps"], n + 1)
                        A(hT2[b].rearrange("p k n -> p (k n)"), ps[:, 4, :], ACT.Copy).then_inc(sm["ht_copied"], 1)
                act.wait_ge(sm["put_free"], l * 16 + 18)
                act.dma_start(x_tok, out_t).then_inc(sm["x_ready"], 16)
            act.wait_ge(sm["x_ready"], 48)

        @block.vector
        def _(dve):
            V = nc.vector
            chain = Chain(dve, sm["dve_step"])
            settle = Settle(dve, sm["settled"])
            mul, add, sub = ALU.mult, ALU.add, ALU.subtract

            chain(V.memset(ones[:, :], 1.0))
            V.memset(toep_sb[:, :, :], 0.0).then_inc(sm["toep_zero"], 1)
            dve.wait_ge(sm["vec_T"], 1)
            V.tensor_copy(vB[:, :], ps[:, 5, 0:B_ROWS]).then_inc(sm["vec_cols"], 1)
            dve.wait_ge(sm["vec_cols"], 1)
            dve.wait_ge(sm["cond_t"], 1)
            cond = small[:, 13, :]
            chain(V.scalar_tensor_tensor(small[:, 14, :], small[:, 0, :], 1.0, vB[:, B_C:B_C + 8], add, mul))
            V.tensor_scalar(cond, small[:, 14, :], 0.5, None, mul).then_inc(sm["cond"], 1)
            dve.wait_ge(sm["cond"], 1)

            for j in range(2):
                for half in range(2):
                    dve.wait_ge(r1_in[2 * j + half], 16)
                    w = ring1[2 * j + half].rearrange("p (k n) -> p k n", k=4)
                    for kk in range(4):
                        k = 4 * half + kk
                        if k == 0:
                            ins = V.tensor_scalar(acc0[j], w[:, kk, :], cond[:, 0:1], None, mul)
                        else:
                            ins = V.scalar_tensor_tensor(acc0[j], w[:, kk, :], cond[:, k:k + 1], acc0[j], mul, add)
                        if kk == 3:
                            ins.then_inc(r1_used[2 * j + half], 1)
                            dve.wait_ge(r1_used[2 * j + half], 1)
                        else:
                            chain(ins)

            def mod_columns(n):
                l, j = divmod(n, 6)
                dve.wait_ge(sm["mod_ps"], n + 1)
                V.tensor_tensor(modc[:, 8 * n:8 * n + 8], ps[:, 7, 8 * n:8 * n + 8], vB[:, 8 * n:8 * n + 8], add) \
                    .then_inc(sm["mod_cols"], 1)
                if j in (1, 4):
                    dve.wait_ge(sm["mod_cols"], n + 1)
                    u = 2 * l + (j == 4)
                    g = (0, 16)[j == 4] + 8 * l
                    V.scalar_tensor_tensor(small[:, 5 + u, :], modc[:, 8 * n:8 * n + 8], 1.0, vA[:, g:g + 8], add, mul) \
                        .then_inc(sm["gain_done"], 1)

            def mean_square(u):
                dve.wait_ge(sm["ss_done"], u + 1)
                chain(V.tensor_scalar(tmp[0], ps[:, 6, :], 1.0 / D, EPS, mul, add))
                V.reciprocal(tmp[0], tmp[0]).then_inc(sm["inv_done"], 1)

            def norm(u):
                if u not in (0, 2):
                    mean_square(u)
                dve.wait_ge(sm["rstd_done"], u + 1)
                for k in range(KC):
                    if u < 4:
                        V.tensor_tensor(hT[:, k, :], xT[:, k, :], tmp[1], mul).then_inc(sm["hn_part"], 1)
                    else:
                        V.scalar_tensor_tensor(hT[:, k, :], xT[:, k, :], vB[:, B_FINAL + k:B_FINAL + k + 1],
                                               tmp[1], mul, mul).then_inc(sm["fin_done"], 1)

            mean_square(0)
            dve.wait_ge(sm["vec_cols"], 2)
            dve.wait_ge(sm["lam"], 2)
            e, z, z2, q = small[:, 2, :], small[:, 11, :], small[:, 12, :], small[:, 14, :]
            chain(V.tensor_scalar(z, e, 2.0, None, add))
            chain(V.reciprocal(z, z))
            chain(V.tensor_tensor(z, z, e, mul))
            chain(V.tensor_tensor(z2, z, z, mul))
            chain(V.tensor_scalar(q, z2, 1.0 / 15, None, mul))
            for n in (13, 11, 9, 7, 5, 3):
                chain(V.scalar_tensor_tensor(q, q, 1.0 / n, z2, add, mul))
            chain(V.scalar_tensor_tensor(q, q, 1.0, z, add, mul))
            chain(V.tensor_scalar(z2, vA[:, 104:112], -1.0, 0.0, mul, ALU.max))
            chain(V.scalar_tensor_tensor(z, q, 2.0, z2, mul, add))
            V.tensor_scalar(small[:, 10, :], z, -2.0, None, mul).then_inc(sm["lru_const"], 1)
            mod_columns(0)
            mod_columns(1)
            dve.wait_ge(sm["gain_done"], 1)
            V.memset(xr[:, :, 0:3], 0.0)
            norm(0)

            with dve.Fori(0, 2) as i:
                n0 = chain.enter(i, 4)
                for b in range(4):
                    c, t = i * 4 + b, tmp[2 + b % 2]
                    g = one(gelu_b[:, bass.ds(c, 1), :])
                    dve.wait_ge(sm["y_sq"], c + 1)
                    chain(V.tensor_scalar(t, t, 0.044715, 1.0, mul, add))
                    V.tensor_tensor(t, t, g, mul).then_inc(sm["y_arg"], 1)
                    dve.wait_ge(sm["y_tanh"], c + 1)
                    V.scalar_tensor_tensor(g, t, 1.0, g, add, mul)
                chain.leave(n0, 2)
            mod_columns(2)
            dve.wait_ge(sm["vec_T"], 3)
            V.tensor_copy(v2[:, :], ps[:, 4, 0:DEPTH * VROWS]).then_inc(sm["vec_cols"], 1)

            def conv(c):
                dve.wait_ge(sm["xi_sb"], c + 1)
                o = one(xc[:, bass.ds(c, 1), :])
                chain(V.tensor_scalar(o, one(xr[:, bass.ds(c, 1), 0:512]), vA[:, bass.ds(c + 48, 1)],
                                      vA[:, bass.ds(c + 80, 1)], mul, add))
                for w in range(1, 4):
                    ins = V.scalar_tensor_tensor(o, one(xr[:, bass.ds(c, 1), w:w + 512]), vA[:, bass.ds(c + (48 + 8 * w), 1)],
                                                 o, mul, add)
                    if w < 3:
                        chain(ins)
                    else:
                        ins.then_inc(sm["conv_done"], 1)

            def recur(h, j):
                c = h * 2 + j
                T = one(xr[:, bass.ds(c, 1), 0:512])
                v = one(gate_v[:, bass.ds(c, 1), :])
                dve.wait_ge(sm["gate_ps"], h * 2 + 2)
                dve.wait_ge(sm["gate_act"], c * 3 + 3)
                V.scalar_tensor_tensor(v, tmp[4 + j], 1.0, one(xc[:, bass.ds(c, 1), :]), add, mul) \
                    .then_inc(sm["gate_free"], 1)
                dve.wait_ge(sm["gate_free"], c + 3)
                chain(V.tensor_scalar(tmp[0], T, -1.0, 1.0, mul, add))
                chain(V.reciprocal(tmp[0], tmp[0]))
                V.tensor_tensor(v, v, tmp[0], mul)
                chain(V.scalar_tensor_tensor(one(xc[:, bass.ds(c, 1), :]), T, 1.0, tmp[0], add, mul))
                V.tensor_scalar(T, T, -1.0, 1e-30, mul, ALU.max).then_inc(sm["neg_done"], 1)

            conv(0)
            conv(1)
            with dve.Fori(0, 2) as h:
                n0 = chain.enter(h, 12)
                conv(h * 2 + 2)
                conv(h * 2 + 3)
                dve.wait_ge(sm["conv_done"], h * 2 + 4)
                recur(h, 0)
                recur(h, 1)
                chain.leave(n0, 2)
            mod_columns(3)
            conv(6)
            conv(7)
            dve.wait_ge(sm["conv_done"], 8)
            for h in (2, 3):
                recur(h, 0)
                recur(h, 1)
            mod_columns(4)
            with dve.Fori(0, KC) as c:
                n0 = chain.enter(c, 2)
                h, v = one(xr[:, bass.ds(c, 1), 0:512]), one(gate_v[:, bass.ds(c, 1), :])
                dve.wait_ge(sm["sqrt_done"], c + 1)
                chain(V.tensor_tensor(v, v, h, mul))
                chain(V.tensor_tensor_scan(h, one(xc[:, bass.ds(c, 1), :]), v, 0.0, mul, add))
                V.scalar_tensor_tensor(one(hT[:, bass.ds(c, 1), :]), h, 0.5, one(gelu_b[:, bass.ds(c, 1), :]), mul, mul).then_inc(sm["z_done"], 1)
                chain.leave(n0, KC)
            for c in range(KC):
                dve.wait_ge(sm["wo_ps"], c + 1)
                t = tmp[2 + c % 2]
                chain(V.tensor_scalar(t, ps[:, c % 4, :], vA[:, 112 + c:113 + c], modc[:, 16 + c:17 + c], add, mul))
                V.tensor_tensor(xT[:, c, :], xT[:, c, :], t, add).then_inc(sm["x_done"], 1)

            for s in (1, 2):
                dve.sem_inc(r1_used[s], 1)

            def ffn(l):
                with dve.Fori(0, 8) as i:
                    for j in range(4):
                        c = i * 4 + j
                        dve.wait_ge(sm["relu_done"], c + (32 * l + 1))
                        V.tensor_tensor(one(u2[:, bass.ds(c, 1), :]), tmp[2 + j % 2], ps[:, j, :], mul).then_inc(sm["u_free"], 1)
                if l == 0:
                    mod_columns(6)
                    mod_columns(7)
                    mod_columns(8)
                else:
                    mod_columns(11)
                    dve.wait_ge(sm["mod_cols"], 12)
                with dve.Fori(0, 2) as i:
                    for b in range(4):
                        c = i * 4 + b
                        x = one(xT[:, bass.ds(c, 1), :])
                        dve.wait_ge(sm["f2_ps"], c + (8 * l + 1))
                        dve.sem_inc(r1_used[(O_FFN[l] + b) % 4], 1)
                        V.scalar_tensor_tensor(x, ps[:, b, :], modc[:, bass.ds(c + (48 * l + 40), 1)], x, mul, add) \
                            .then_inc(sm["x_done"], 1)

            mod_columns(5)
            norm(1)
            ffn(0)
            mean_square(2)
            chain(V.tensor_tensor(small[:, 9, :], modc[:, 64:72], vA[:, 120:128], mul))
            V.memset(hp[:, :, 0:PAD], 0.0)
            for i in range(2):
                V.memset(pw[i][:, :, 0:PAD], 0.0)
            norm(2)
            mod_columns(9)
            mod_columns(10)
            for g, win in enumerate(WINDOWS):
                dve.wait_ge(sm["h_done"], 16 + 2 * g + 2)
                if g >= 1:
                    dve.wait_ge(sm["pool_done"], g)
                src = x0 = hp[:, 2 * g:2 * g + 2, :]
                w, n = 1, 0
                while w < win:
                    dst = pw[n % 2]
                    chain(V.tensor_tensor(dst[:, :, PAD:], src[:, :, PAD:], src[:, :, PAD - w:PAD + S - w], add))
                    src, w, n = dst, 2 * w, n + 1
                inv = const[:, C_INV + 16 * g:C_INV + 16 * g + 16].unsqueeze(1).to_broadcast([P, 2, 16])
                V.scalar_tensor_tensor(hT[:, 2 * g:2 * g + 2, 16:], src[:, :, PAD + 16:], 1.0 / win,
                                       x0[:, :, PAD + 16:], mul, sub)
                chain(V.tensor_tensor(src[:, :, PAD:PAD + 16], src[:, :, PAD:PAD + 16], inv, mul))
                V.tensor_tensor(hT[:, 2 * g:2 * g + 2, 0:16], src[:, :, PAD:PAD + 16], x0[:, :, PAD:PAD + 16], sub) \
                    .then_inc(sm["pool_done"], 1)
            for c in range(KC):
                dve.wait_ge(sm["wp_ps"], c + 1)
                V.scalar_tensor_tensor(xT[:, c, :], ps[:, c % 4, :], small[:, 9, c:c + 1], xT[:, c, :], mul, add) \
                    .then_inc(sm["x_done"], 1)
            dve.sem_inc(r1_used[0], 1)
            norm(3)
            ffn(1)
            norm(4)
            for t in range(TC):
                for half in range(2):
                    n = 2 * t + half
                    dve.wait_ge(sm["fin_T"], n + 1)
                    ins = V.tensor_copy(x_tok[:, t, 512 * half:512 * half + 512], ps[:, n % 4, :])
                    ins.then_inc(sm["fin_copied"], 1)
            dve.wait_ge(sm["fin_copied"], 8)
            chain(V.memset(st[:, 156:157], 0.0))
            V.tensor_copy(st[:, 157:158], st[:, 156:157]).then_inc(sm["x_ready"], 16)

            with dve.Fori(0, DEPTH) as l:
                c0 = chain.enter(l, DVE_LAYER)
                gain = st[:, 96:96 + VROWS]

                def norm2(w):
                    dve.wait_ge(sm["n_ss"], l * 8 + (4 * w + 4))
                    chain(V.tensor_scalar(st[:, 4:8], st[:, 0:4], 1.0 / D, EPS, mul, add))
                    V.reciprocal(st[:, 4:8], st[:, 4:8]).then_inc(sm["n_inv"], 1)
                    dve.wait_ge(sm["n_rstd"], l * 2 + (w + 1))
                    for t in range(TC):
                        V.tensor_scalar(xn[:, t, :], x_tok[:, t, :], st[:, 8 + t:9 + t], None, mul).then_inc(sm["xn_done"], 1)

                norm2(0)
                dve.wait_ge(sm["proj_copied"], l * 16 + 16)
                chain(V.tensor_tensor(p3sq, p3[:, :, 0:384], p3[:, :, 0:384], mul))
                V.tensor_reduce(st[:, 16:20], p3sq[:, :, 0:QR], AX.X, add)
                chain(V.tensor_reduce(st[:, 20:24], p3sq[:, :, QR:], AX.X, add))
                V.tensor_scalar(st[:, 16:20], st[:, 16:20], 1.0 / QR, EPS, mul, add)
                chain(V.tensor_scalar(st[:, 20:24], st[:, 20:24], 1.0 / KVR, EPS, mul, add))
                V.reciprocal(st[:, 16:24], st[:, 16:24]).then_inc(sm["c_ss"], 1)
                dve.wait_ge(sm["c_r"], l + 1)
                for t in range(TC):
                    V.tensor_scalar(p3[:, t, 0:QR], p3[:, t, 0:QR], st[:, 24 + t:25 + t], None, mul)
                    V.tensor_scalar(p3[:, t, QR:384], p3[:, t, QR:384], st[:, 28 + t:29 + t], None, mul).then_inc(sm["c_normed"], 1)
                for h in range(B_HEADS):
                    ins = V.tensor_copy(kb[:, :, h, NOPE:], p3[:, :, 384:416])
                ins.then_inc(sm["kr_copied"], 1)

                qa12 = qk.rearrange("p t (h d) -> p (t h) d", d=HD)
                chain(V.tensor_tensor(normsq, qk.rearrange("p t d -> p (t d)"), qk.rearrange("p t d -> p (t d)"), mul))
                chain(V.tensor_reduce(st[:, 48:96], normsq.rearrange("p (h d) -> p h d", d=HD), AX.X, add))
                chain(V.tensor_scalar(st[:, 48:96], st[:, 48:96], 1.0 / HD, EPS, mul, add))
                V.reciprocal(st[:, 48:96], st[:, 48:96]).then_inc(sm["qk_ss"], 1)
                dve.wait_ge(sm["qk_r"], l * 2 + 1)
                chain(V.tensor_tensor(qa12, qa12, st[:, 48:96].unsqueeze(2).to_broadcast([P, 48, HD]), mul))
                dve.wait_ge(sm["p2_copied"], l * 16 + 16)
                sq = normsq[:, 0:2304]
                for i, x in enumerate((qb, kb)):
                    flat = x.rearrange("p t h d -> p (t h d)")
                    chain(V.tensor_tensor(sq, flat, flat, mul))
                    chain(V.tensor_reduce(st[:, 48 + 24 * i:72 + 24 * i], sq.rearrange("p (h d) -> p h d", d=QK), AX.X, add))
                chain(V.tensor_scalar(st[:, 48:96], st[:, 48:96], 1.0 / QK, EPS, mul, add))
                V.reciprocal(st[:, 48:96], st[:, 48:96]).then_inc(sm["qk_ss"], 1)
                dve.wait_ge(sm["qk_r"], l * 2 + 2)
                for i, x in enumerate((qb, kb)):
                    v = x.rearrange("p t h d -> p (t h) d")
                    chain(V.tensor_tensor(v, v, st[:, 48 + 24 * i:72 + 24 * i].unsqueeze(2).to_broadcast([P, 24, QK]), mul))
                    g = qkg[:, i, bass.ds(l, 1), :].to_broadcast([P, 24, QK])
                    chain(V.tensor_tensor(v, v, g, mul))
                    x1, x2 = x[:, :, :, NOPE:NOPE + 16], x[:, :, :, NOPE + 16:]
                    cos = const[:, C_COS:C_COS + 64].rearrange("p (t n) -> p t n", t=TC).unsqueeze(2).to_broadcast([P, TC, B_HEADS, 16])
                    sin = const[:, C_SIN:C_SIN + 64].rearrange("p (t n) -> p t n", t=TC).unsqueeze(2).to_broadcast([P, TC, B_HEADS, 16])
                    V.tensor_tensor(ropet[0], x1, cos, mul)
                    V.tensor_tensor(ropet[1], x2, sin, mul)
                    V.tensor_tensor(ropet[2], x2, cos, mul)
                    chain(V.tensor_tensor(ropet[3], x1, sin, mul))
                    V.tensor_tensor(x1, ropet[0], ropet[1], sub)
                    ins = V.tensor_tensor(x2, ropet[2], ropet[3], add)
                    if i == 0:
                        chain(ins)
                    else:
                        ins.then_inc(sm["qk_normed"], 1)

                V.memset(cu[:, :, 0:1], 0.0)
                V.memset(cu[:, :, 513:514], 0.0)
                for j in range(2):
                    dve.wait_ge(sm["conv_copied"], l * 6 + (3 * j + 3))
                    chain(V.tensor_tensor(cu[:, j, 1:513], cv[:, 4 + j, :], cv[:, j, :], mul))
                    w = [gain[:, G_CONV + 2 * k + j:G_CONV + 2 * k + j + 1] for k in range(3)]
                    chain(V.tensor_scalar(oc[:, j, :], cu[:, j, 0:512], w[0], None, mul))
                    chain(V.scalar_tensor_tensor(oc[:, j, :], cu[:, j, 1:513], w[1], oc[:, j, :], mul, add))
                    chain(V.scalar_tensor_tensor(oc[:, j, :], cu[:, j, 2:514], w[2], oc[:, j, :], mul, add))
                    chain(V.tensor_tensor(oc[:, j, :], oc[:, j, :], cv[:, 2 + j, :], mul))
                    V.tensor_tensor(cvs[:, j, :], oc[:, j, :], oc[:, j, :], mul).then_inc(sm["conv_sq"], 1)
                dve.wait_ge(sm["conv_sq"], l * 2 + 2)
                V.memset(kT[HD:P, 0, :], 0.0)
                V.memset(kT[0:HD, 1, :], 0.0).then_inc(sm["conv_out"], 1)
                dve.wait_ge(sm["cs_ps"], l + 1)
                chain(V.tensor_scalar(cvs[:, 0, :], ps[:, 6, :], 1.0 / CONV, EPS, mul, add))
                V.reciprocal(cvs[:, 0, :], cvs[:, 0, :]).then_inc(sm["c_inv"], 1)
                dve.wait_ge(sm["c_rstd"], l + 1)
                V.scalar_tensor_tensor(oc[:, 0, :], oc[:, 0, :], gain[:, G_OUT + 6:G_OUT + 7], cvs[:, 1, :], mul, mul)
                chain(V.scalar_tensor_tensor(oc[:, 1, :], oc[:, 1, :], gain[:, G_OUT + 7:G_OUT + 8], cvs[:, 1, :], mul, mul))

                def heads(kind):
                    settle()
                    with dve.Fori(0, 3) as p:
                        n1 = chain.enter(p, 16)
                        n = l * 48 + p * 8 + kind * 24

                        def out_tile(i):
                            hh, t = divmod(i, 4)
                            dve.wait_ge(sm["o_ps"], n + (i + 1))
                            if kind == 0:
                                dst = one(qk[:, t:t + 1, bass.ds(p * 128 + 64 * hh, 64)])
                            else:
                                dst = one(qb[:, t, bass.ds(p * 2 + hh, 1), 0:VD])
                            V.tensor_scalar(dst, ps[:, 6 + i % 2, 0:64], st[:, 144 + i:145 + i], None, mul) \
                                .then_inc(sm["o_done"], 1)

                        for i in range(8):
                            hh, t = divmod(i, 4)
                            dve.wait_ge(sm["s_ps"], n + (i + 1))
                            if kind == 0:
                                if t == 0:
                                    dve.wait_ge(sm["bias_ready"], l * 6 + p * 2 + (hh + 1))
                                b = bias[hh][:, 6 - 2 * t:14 - 2 * t, 0:GRID]
                                sc = prob[:, i % 2, :].rearrange("p (r n) -> p r n", n=GRID)
                                ins = V.scalar_tensor_tensor(sc, ps[:, i % 2, :].rearrange("p (r n) -> p r n", n=GRID),
                                                             HD ** -0.5, b, mul, add)
                                chain(ins)
                                if t == 3:
                                    V.tensor_copy(st[:, 157:158], st[:, 156:157]).then_inc(sm["bias_used"], 1)
                                V.tensor_reduce(st[:, 32 + i:33 + i], prob[:, i % 2, :], AX.X, ALU.max, negate=True) \
                                    .then_inc(sm["s_max"], 1)
                            else:
                                chain(V.tensor_reduce(st[:, 32 + i:33 + i], ps[:, i % 2, :], AX.X, ALU.max, negate=True))
                                V.tensor_scalar(st[:, 32 + i:33 + i], st[:, 32 + i:33 + i], QK ** -0.5, None, mul) \
                                    .then_inc(sm["s_max"], 1)
                            if i >= 1:
                                dve.wait_ge(sm["p_done"], n + i)
                                chain(V.reciprocal(st[:, 143 + i:144 + i], st[:, 39 + i:40 + i]))
                            if i >= 3:
                                out_tile(i - 3)
                        dve.wait_ge(sm["p_done"], n + 8)
                        chain(V.reciprocal(st[:, 151:152], st[:, 47:48]))
                        for i in (5, 6, 7):
                            out_tile(i)
                        chain.leave(n1, 3)

                heads(0)
                dve.sem_inc(r2_used[3], 1)
                heads(1)

                dve.wait_ge(sm["o_done"], l * 48 + 48)
                va_out = qk[:, :, 0:A_W].rearrange("p t (h d) -> p t h d", h=6)
                vb_out = qb[:, :, :, 0:VD]
                for i, x in enumerate((va_out, vb_out)):
                    chain(V.tensor_tensor(mix_sq, x, x, mul))
                    chain(V.tensor_reduce(st[:, 16 + 4 * i:20 + 4 * i], mix_sq.rearrange("p t h d -> p t (h d)"), AX.X, add))
                chain(V.tensor_scalar(st[:, 16:24], st[:, 16:24], 1.0 / A_W, EPS, mul, add))
                V.reciprocal(st[:, 16:24], st[:, 16:24]).then_inc(sm["m_ss"], 1)
                dve.wait_ge(sm["m_r"], l + 1)
                for i, x in enumerate((va_out, vb_out)):
                    for t in range(TC):
                        ins = V.tensor_scalar(mix_tok[:, t, A_W * i:A_W * i + A_W].rearrange("p (h d) -> p h d", h=6),
                                              x[:, t], st[:, 16 + 4 * i + t:17 + 4 * i + t], None, mul)
                    ins.then_inc(sm["m_normed"], 1)
                V.tensor_copy(hnT[:, 6:8, :], oc).then_inc(sm["m_normed"], 1)
                chain(V.tensor_copy(wr_l.rearrange("p k e -> p (k e)"),
                                    wr[:, bass.ds(l, 1), :, :].rearrange("p a k e -> p (a k e)")))
                for n in range(8):
                    t, half = divmod(n, 2)
                    x = x_tok[:, t, 512 * half:512 * half + 512]
                    dve.wait_ge(sm["wout_ps"], l * 8 + (n + 1))
                    V.tensor_tensor(x, x, ps[:, n % 4, :], add).then_inc(sm["x_added"], 1)
                for s in (4, 5):
                    dve.sem_inc(r2_used[s], 1)
                norm2(1)

                dve.wait_ge(sm["lg_ps"], l * 2 + 1)
                V.tensor_copy(lg_T[0:EXPERTS], ps[0:EXPERTS, 6, :]).then_inc(sm["lt_sb"], 1)
                dve.wait_ge(sm["lg_ps"], l * 2 + 2)
                b = br[:, bass.ds(l, 1), :].to_broadcast([P, TC, EXPERTS])
                chain(V.tensor_tensor(lg, ps[:, 7, 0:64].rearrange("p (t e) -> p t e", t=TC), b, add))
                chain(V.tensor_reduce(st[:, 12:16], lg, AX.X, ALU.max))
                V.tensor_tensor(lg, lg, st[:, 12:16].unsqueeze(2).to_broadcast([P, TC, EXPERTS]), sub).then_inc(sm["lg_max"], 1)
                dve.wait_ge(sm["lg_exp"], l + 1)
                chain(V.tensor_reduce(st[:, 12:16], lg, AX.X, add))
                chain(V.reciprocal(st[:, 12:16], st[:, 12:16]))
                V.tensor_tensor(lg, lg, st[:, 12:16].unsqueeze(2).to_broadcast([P, TC, EXPERTS]), mul).then_inc(sm["aff_done"], 1)
                dve.wait_ge(sm["aff_ps"], l + 1)
                chain(V.tensor_copy(aff[0:EXPERTS], ps[0:EXPERTS, 7, :]))
                for r in range(CAP // 8):
                    src, dst = (aff, aff2) if r % 2 == 0 else (aff2, aff)
                    v8 = top_v[0:EXPERTS, 8 * r:8 * r + 8]
                    settle()
                    chain(V.max(v8, src[0:EXPERTS]))
                    settle()
                    ins = V.max_index(top_i[0:EXPERTS, 8 * r:8 * r + 8], v8, src[0:EXPERTS])
                    if r < CAP // 8 - 1:
                        ins = V.match_replace(dst[0:EXPERTS], v8, src[0:EXPERTS], -1.0)
                    chain(ins)
                V.tensor_copy(top_v[0:EXPERTS, CAP:], top_v[0:EXPERTS, 0:CAP])
                chain(V.tensor_copy(idx_f[0:EXPERTS, 128:192], top_i[0:EXPERTS]))
                V.tensor_scalar(idx_f[0:EXPERTS, 0:64], idx_f[0:EXPERTS, 128:192], 2.0, None, mul)
                V.tensor_scalar(idx_f[0:EXPERTS, 64:128], idx_f[0:EXPERTS, 128:192], 2.0, 1.0, mul, add).then_inc(sm["idx_done"], 1)
                dve.wait_ge(sm["idx_ps"], l + 1)
                V.tensor_copy(gate_t, ps[:, 6, 64:80])
                V.tensor_copy(put_i, ps[:, 6, 80:96])
                V.tensor_copy(get_i[0:CAP], ps[0:CAP, 6, 96:112]).then_inc(sm["idx_cols"], 1)
                dve.wait_ge(sm["idx_cols"], l + 1)

                settle()
                with dve.Fori(0, EXPERTS // 2) as i:
                    n1 = chain.enter(i, 2)
                    for b in range(2):
                        n = l * 16 + i * 2 + b
                        dve.wait_ge(sm["xst_ps"], n + 1)
                        V.tensor_tensor(xsT[b], ps[:, 5, :].rearrange("p (k n) -> p k n", k=KC),
                                        gain[:, G_FFN:G_FFN + 8].unsqueeze(2).to_broadcast([P, KC, CAP]), mul) \
                            .then_inc(sm["xs_ready"], 1)
                        dve.wait_ge(sm["g_tanh"], n + 1)
                        chain(V.scalar_tensor_tensor(hid[b], hidt[b], 1.0, ps[:, 2 * b, :], add, mul))
                        dve.wait_ge(sm["u_ps"], n + 1)
                        dve.sem_inc(r2_used[3], 1)
                        V.scalar_tensor_tensor(hid[b], hid[b], 0.5, ps[:, 2 * b + 1, :], mul, mul).then_inc(sm["hid_done"], 1)
                        dve.wait_ge(sm["y2_ps"], n + 1)
                        dve.sem_inc(r2_used[5], 1)
                        dve.wait_ge(sm["put_free"], n + 1)
                        V.tensor_scalar(ye[b], ps[:, 6 + b, :], gate_t[:, bass.ds(i * 2 + b, 1)], None, mul) \
                            .then_inc(sm["ye_done"], 1)
                    chain.leave(n1, 8)
                chain.leave(c0, DEPTH)

        @block.tensor
        def _(pe):
            mm, tr = nc.tensor.matmul, nc.tensor.transpose
            settle = Settle(pe, sm["settled"])

            pe.wait_ge(sm["const_in"], 16)
            pe.wait_ge(sm["vecB_in"], 48)
            tr(ps[:, 5, 0:B_ROWS], vrow[0:B_ROWS, 1, :], ident[0:B_ROWS, 0:B_ROWS]).then_inc(sm["vec_T"], 1)
            pe.wait_ge(sm["x_in"], 16)
            for k in range(KC):
                if k >= 4:
                    pe.wait_ge(sm["x_done"], k - 3)
                for t in range(TC):
                    ins = tr(ps[:, k % 4, P * t:P * t + P], x_rows[:, t, P * k:P * k + P], ident)
                ins.then_inc(sm["xr_T"], 1)
            pe.wait_ge(sm["vecA_in"], 16 * len(ROW_A))
            tr(ps[:, 4, 0:P], vrow[:, 0, :], ident).then_inc(sm["vec_T"], 1)

            def mod_sum(n):
                src = acc0[n] if n < 2 else mod_acc[n % 2]
                if n >= 1:
                    pe.wait_ge(sm["mod_cols"], n)
                if n < 2:
                    pe.wait_ge(r1_used[2 * n + 1], 1)
                else:
                    pe.wait_ge(sm["mod_sum"], n - 1)
                for k in range(KC):
                    ins = mm(ps[:, 7, 8 * n + k:8 * n + k + 1], src[:, P * k:P * k + P], ones[:, 0:1], start=True, stop=True)
                ins.then_inc(sm["mod_ps"], 1)

            def norm(u):
                for k in range(KC):
                    pe.wait_ge(sm["sq_done"], 8 * u + k + 1)
                    ins = mm(ps[:, 6, :], ones[:, :], squares[u][:, k, :], start=(k == 0), stop=(k == KC - 1))
                ins.then_inc(sm["ss_done"], 1)

            def dense(name, slots, fill, u, freed, base=0):
                if u is None:
                    pe.wait_ge(r1_in[slots[0]], 16 * (fill + 1))
                    w = ring1[slots[0]].rearrange("p (k n) -> p k n", k=KC)
                    for k in range(KC):
                        pe.wait_ge(sm["z_done"], k + 1)
                        for c in range(4):
                            ins = mm(ps[:, c, :], w[:, k, P * c:P * c + P], hT[:, k, :], start=(k == 0), stop=(k == KC - 1))
                            if k == KC - 1:
                                ins.then_inc(sm[name], 1)
                for c in range(4 if u is None else 0, KC):
                    s = slots[c // 4]
                    if c % 4 == 0:
                        pe.wait_ge(r1_in[s], 16 * (fill + 1))
                    if c >= 4:
                        pe.wait_ge(sm[freed], base + c - 3)
                    w = ring1[s].rearrange("p (k n) -> p k n", k=KC)
                    for k in range(KC):
                        if c == 0:
                            pe.wait_ge(sm["h_done"], 8 * u + k + 1)
                        ins = mm(ps[:, c % 4, :], w[:, k, P * (c % 4):P * (c % 4) + P], hT[:, k, :],
                                 start=(k == 0), stop=(k == KC - 1))
                    ins.then_inc(sm[name], 1)

            norm(0)
            mod_sum(0)
            mod_sum(1)
            dense("y_ps", (0, 1), 1, 0, "y_sb")
            mod_sum(2)
            n = DEPTH * VROWS
            pe.wait_ge(sm["vec2_in"], 16 * DEPTH * 10)
            tr(ps[:, 4, 0:n], vrow[0:n, 2, :], ident[0:n, 0:n]).then_inc(sm["vec_T"], 1)
            pe.wait_ge(sm["y_sb"], 8)
            pe.wait_ge(sm["vec_cols"], 3)

            def x_in(c):
                s = 2 + c // 4
                if c % 4 == 0:
                    pe.wait_ge(r1_in[s], 32)
                if c >= 2:
                    pe.wait_ge(sm["xi_sb"], c - 1)
                w = ring1[s].rearrange("p (k n) -> p k n", k=KC)
                for k in range(KC):
                    ins = mm(ps[:, c % 2, :], w[:, k, P * (c % 4):P * (c % 4) + P], hT[:, k, :],
                             start=(k == 0), stop=(k == KC - 1))
                ins.then_inc(sm["xi_ps"], 1)

            wg = ring1[0].rearrange("p (g h i n) -> p g h i n", g=2, h=4, i=2)

            def gates(c):
                h, j = divmod(c, 2)
                if c == 0:
                    pe.wait_ge(r1_in[0], R1_IN(0, 2))
                pe.wait_ge(sm["conv_done"], 2 * h + 2)
                if c >= 2:
                    pe.wait_ge(sm["gate_act"], 3 * (c - 1))
                for g in range(2):
                    for i in range(2):
                        ins = mm(ps[:, 2 + 2 * (c % 2) + g, :], wg[:, g, h, i, P * j:P * j + P], xc[:, 2 * h + i, :],
                                 start=(i == 0), stop=(i == 1))
                ins.then_inc(sm["gate_ps"], 1)

            x_in(0)
            x_in(1)
            for h in range(4):
                for j in range(2):
                    if h < 3:
                        x_in(2 * h + 2 + j)
                for j in range(2):
                    gates(2 * h + j)
                if h == 1:
                    mod_sum(3)
            mod_sum(4)
            pe.wait_ge(sm["gate_act"], 24)
            dense("wo_ps", (1, 2), 2, None, "x_done", 8)

            def ffn(l):
                f0, o = F_FFN[l], O_FFN[l]
                def first(i):
                    for b in range(4):
                        s = (o + b) % 4
                        pe.wait_ge(r1_in[s], i * 16 + R1_IN(s, f0[s]))
                        w = ring1[s].rearrange("p (k n) -> p k n", k=KC)
                        for j in range(4):
                            pe.wait_ge(sm["u_free"], i * 16 + (32 * l + 4 * b + j + 1))
                            for k in range(KC):
                                if b == 0 and j == 0:
                                    pe.wait_ge(sm["h_done"], 8 * (2 * l + 1) + k + 1)
                                ins = mm(ps[:, j, :], w[:, k, P * j:P * j + P], hT[:, k, :], start=(k == 0), stop=(k == KC - 1))
                            ins.then_inc(sm["f1_ps"], 1)

                if l == 0:
                    first(0)
                    mod_sum(6)
                    first(1)
                    mod_sum(7)
                    mod_sum(8)
                else:
                    with pe.Fori(0, 2) as i:
                        first(i)
                    mod_sum(11)
                pe.wait_ge(sm["u_free"], 32 * l + 36)
                with pe.Fori(0, 2) as i:
                    for b in range(4):
                        s = (o + b) % 4
                        pe.wait_ge(r1_in[s], i * 16 + R1_IN(s, f0[s] + 2))
                        pe.wait_ge(sm["x_done"], i * 4 + (16 + 16 * l + b - 3))
                        w = ring1[s].rearrange("p (k n) -> p k n", k=FC)
                        for f in range(FC):
                            ins = mm(ps[:, b, :], w[:, f, :], u2[:, f, :], start=(f == 0), stop=(f == FC - 1))
                        ins.then_inc(sm["f2_ps"], 1)

            mod_sum(5)
            norm(1)
            ffn(0)
            norm(2)
            mod_sum(9)
            mod_sum(10)
            pe.wait_ge(r1_in[0], R1_IN(0, 7))
            wp = ring1[0][:, 0:2048].rearrange("p (g i n) -> p g i n", g=4, i=2)
            for c in range(KC):
                g, j = divmod(c, 2)
                pe.wait_ge(sm["pool_done"], g + 1)
                if c >= 4:
                    pe.wait_ge(sm["x_done"], 24 + c - 3)
                for i in range(2):
                    ins = mm(ps[:, c % 4, :], wp[:, g, i, P * j:P * j + P], hT[:, 2 * g + i, :], start=(i == 0), stop=(i == 1))
                ins.then_inc(sm["wp_ps"], 1)
            norm(3)
            ffn(1)
            norm(4)
            for t in range(TC):
                for half in range(2):
                    n = 2 * t + half
                    if n >= 4:
                        pe.wait_ge(sm["fin_copied"], n - 3)
                    for k in range(4):
                        pe.wait_ge(sm["fin_done"], 4 * half + k + 1)
                        ins = tr(ps[:, n % 4, P * k:P * k + P], hT[:, 4 * half + k, P * t:P * t + P], ident)
                    ins.then_inc(sm["fin_T"], 1)

            pe.wait_ge(sm["gains_in"], 16 * 8)
            with pe.Fori(0, DEPTH) as l:

                def norm2(w):
                    pe.wait_ge(sm["xn_done"], l * 8 + (4 * w + 4))
                    for k in range(KC + w):
                        if k >= 2:
                            pe.wait_ge(sm["hn_ready"], l * 16 + (8 * w + k - 1))
                        if k < KC:
                            for t in range(TC):
                                ins = tr(ps[:, 4 + k % 2, P * t:P * t + P], xn[:, t, P * k:P * k + P], ident)
                            ins.then_inc(sm["xt_ps"], 1)
                        if w == 1 and k >= 1:
                            pe.wait_ge(sm["hn_ready"], l * 16 + (8 + k))
                            ins = mm(ps[0:EXPERTS, 6, :], wr_l[:, k - 1, :], hnT[:, k - 1, :], start=(k == 1), stop=(k == KC))
                    if w == 1:
                        ins.then_inc(sm["lg_ps"], 1)

                def landed(s, n):
                    pe.wait_ge(r2_in[s], l * R2_IN[s] + 16 * n)

                def used(s, name, value):
                    pe.wait_ge(sm[name], value)
                    pe.sem_inc(r2_used[s], 1)

                norm2(0)
                pe.wait_ge(sm["hn_ready"], l * 16 + 8)
                for j in range(4):
                    n = 384 if j < 3 else 416
                    landed(j, 2 if j < 3 else 1)
                    w = ring2[j][:, 0:KC * n].rearrange("p (k n) -> p k n", k=KC)
                    for t in range(TC):
                        if j >= 1:
                            pe.wait_ge(sm["proj_copied"], l * 16 + (4 * j + t - 3))
                        for k in range(KC):
                            ins = mm(ps[:, t, 0:n], hnT[:, k, P * t:P * t + P], w[:, k, :], start=(k == 0), stop=(k == KC - 1))
                        ins.then_inc(sm["proj_ps"], 1)
                pe.wait_ge(sm["c_normed"], l * 4 + 4)
                for i in range(3):
                    for t in range(TC):
                        ins = tr(ps[:, 4 + i, P * t:P * t + P], p3[:, t, P * i:P * i + P], ident)
                    ins.then_inc(sm["ct_ps"], 1)
                pe.wait_ge(sm["ct_copied"], l * 3 + 3)
                for t in range(TC):
                    for i in range(4):
                        if t == 0:
                            pe.wait_ge(sm["proj_copied"], l * 16 + (13 + i))
                        else:
                            pe.wait_ge(sm["p2_copied"], l * 16 + (4 * t + i - 3))
                        if i < 2:
                            for k in range(2):
                                ins = mm(ps[:, i, 0:288], cT[:, k, P * t:P * t + P], ring2[1 + k][:, 3072 + 288 * i:3360 + 288 * i],
                                         start=(k == 0), stop=(k == 1))
                        else:
                            ins = mm(ps[:, i, 0:384], cT[:, 2, P * t:P * t + P], ring2[0][:, 3072 + 384 * (i - 2):3456 + 384 * (i - 2)],
                                     start=True, stop=True)
                        ins.then_inc(sm["p2_ps"], 1)
                for c in range(6):
                    s, j = divmod((0, 4, 2, 1, 5, 3)[c], 3)
                    s += 4
                    if c < 2:
                        landed(s, 1)
                    if c >= 4:
                        pe.wait_ge(sm["conv_copied"], l * 6 + (c - 3))
                    w = ring2[s][:, 0:3072].rearrange("p (k n) -> p k n", k=KC)
                    for k in range(KC):
                        ins = mm(ps[:, 4 + c % 4, :], w[:, k, P * j:P * j + P], hnT[:, k, :], start=(k == 0), stop=(k == KC - 1))
                    ins.then_inc(sm["conv_ps"], 1)
                pe.wait_ge(sm["conv_sq"], l * 2 + 2)
                for s, name, value in ((0, "p2_ps", l * 16 + 16), (1, "p2_ps", l * 16 + 16),
                                       (2, "p2_ps", l * 16 + 16), (4, "conv_ps", l * 6 + 6), (5, "conv_ps", l * 6 + 6)):
                    used(s, name, value)
                for j in range(2):
                    ins = mm(ps[:, 6, :], ones[:, :], cvs[:, j, :], start=(j == 0), stop=(j == 1))
                ins.then_inc(sm["cs_ps"], 1)

                def stage(kind, p, dp, steps):
                    m = l * 18 + p * (2, 4)[kind] + (0, 6)[kind] + (2, 4)[kind] * dp
                    for i in steps:
                        if i == 0:
                            pe.wait_ge(sm["staged"], l * 12 + p * 2 + (6 * kind + 2 * dp + 2))
                        if i >= 2:
                            pe.wait_ge(sm["st_copied"], m + (i - 1))
                        for t in range(TC):
                            if kind == 0:
                                src = (stage_qa, stage_ka)[i][:, t, :]
                                ins = mm(ps[:, 4 + i, P * t:P * t + P], src, (flip, ident)[i], start=True, stop=True)
                            else:
                                src = (stage_q, stage_k)[i // 2][:, t, i % 2, :]
                                ins = tr(ps[0:QK, 4 + i % 2, P * t:P * t + P], src, ident)
                        ins.then_inc(sm["st_T"], 1)

                def pair(kind, p, following):
                    v = (va, vb)[kind]
                    n = l * 48 + p * 8 + kind * 24
                    pe.wait_ge(sm["st_copied"], l * 18 + p * (2, 4)[kind] + ((0, 6)[kind] + (2, 4)[kind]))
                    def scores(i):
                        hh, t = divmod(i, 4)
                        if kind == 0:
                            q, k = qT[:, 0], kT[:, hh]
                        else:
                            q, k = (x[0:QK, hh] for x in (qT, kT))
                        mm(ps[:, i % 2, :], q[:, P * t:P * t + P], k, start=True, stop=True).then_inc(sm["s_ps"], 1)

                    scores(0)
                    for i in range(9):
                        if i < 7:
                            scores(i + 1)
                        if i == 7 and following:
                            stage(*following, range(2))
                        if i == 8 and following and following[0] == 1:
                            stage(*following, range(2, 4))
                        if i < 8:
                            pe.wait_ge(sm["p_done"], n + (i + 1))
                            for k in range(TC):
                                ins = tr(ps[:, 2 + i % 2, P * k:P * k + P], prob[:, i % 2, P * k:P * k + P], ident)
                            ins.then_inc(sm["pt_ps"], 1)
                        if i >= 1:
                            hh, t = divmod(i - 1, 4)
                            pe.wait_ge(sm["pt_copied"], n + i)
                            if i >= 3:
                                pe.wait_ge(sm["o_done"], n + (i - 2))
                            for k in range(TC):
                                ins = mm(ps[:, 6 + (i - 1) % 2, 0:64], probT[:, (i - 1) % 2, P * k:P * k + P],
                                         one(v[:, k:k + 1, bass.ds(p * 128 + 64 * hh, 64)]),
                                         start=(k == 0), stop=(k == TC - 1))
                            ins.then_inc(sm["o_ps"], 1)

                stage(0, 0, 0, range(2))
                for kind in range(2):
                    settle()
                    with pe.Fori(0, 2) as p:
                        pair(kind, p, (kind, p, 1))
                    pair(kind, 2, (1, 0, 0) if kind == 0 else None)
                for c in range(6):
                    pe.wait_ge(sm["m_normed"], l * 3 + (1 + c // 3))
                    if c >= 2:
                        pe.wait_ge(sm["mt_copied"], l * 6 + (c - 1))
                    for t in range(TC):
                        src = mix_tok[:, t, P * c:P * c + P]
                        ins = mm(ps[:, 4 + c % 2, P * t:P * t + P], src, (flip, ident)[c // 3], start=True, stop=True)
                    ins.then_inc(sm["mt_ps"], 1)
                pe.wait_ge(sm["mt_copied"], l * 6 + 6)
                pe.wait_ge(sm["m_normed"], l * 3 + 3)
                landed(4, 2)
                landed(5, 2)
                for n in range(8):
                    t, half = divmod(n, 2)
                    if n >= 4:
                        pe.wait_ge(sm["x_added"], l * 8 + (n - 3))
                    for k in range(KC):
                        w = ring2[4 + k // 4].rearrange("p (k n) -> p k n", k=4)
                        ins = mm(ps[:, n % 4, :], hnT[:, k, P * t:P * t + P], w[:, k % 4, 512 * half:512 * half + 512],
                                 start=(k == 0), stop=(k == KC - 1))
                    ins.then_inc(sm["wout_ps"], 1)
                norm2(1)
                pe.wait_ge(sm["lt_sb"], l + 1)
                settle()
                for t in range(TC):
                    ins = tr(ps[:, 7, EXPERTS * t:EXPERTS * t + EXPERTS], lg_T[0:EXPERTS, P * t:P * t + P],
                             ident[0:EXPERTS, 0:EXPERTS])
                ins.then_inc(sm["lg_ps"], 1)
                pe.wait_ge(sm["aff_done"], l + 1)
                for t in range(TC):
                    ins = tr(ps[0:EXPERTS, 7, P * t:P * t + P], lg[:, t, :], ident)
                ins.then_inc(sm["aff_ps"], 1)
                pe.wait_ge(sm["idx_done"], l + 1)
                settle()
                tr(ps[:, 6, 64:80], top_v[0:EXPERTS, :], ident[0:EXPERTS, 0:EXPERTS])
                tr(ps[:, 6, 80:96], idx_f[0:EXPERTS, 0:128], ident[0:EXPERTS, 0:EXPERTS])
                tr(ps[0:CAP, 6, 96:112], idx_f[0:EXPERTS, 128:192], ident[0:EXPERTS, 0:EXPERTS]).then_inc(sm["idx_ps"], 1)
                pe.wait_ge(sm["idx_cols"], l + 1)

                settle()
                with pe.Fori(0, EXPERTS // 2) as i:
                    for b in range(2):
                        n = l * 16 + i * 2 + b
                        pe.wait_ge(got[b], l * 128 + i * 16 + 16)
                        settle()
                        for k in range(KC):
                            ins = tr(ps[:, 5, CAP * k:CAP * k + CAP], xg[b][0:CAP, P * k:P * k + P], ident[0:CAP, 0:CAP])
                        ins.then_inc(sm["xst_ps"], 1)
                        pe.wait_ge(sm["xs_ready"], n + 1)

                        def halves(bank, lhs, s, first, last):
                            if s < 2 or s >= 6:
                                r2 = l * R2_IN[s] + i * 16 + R2_BASE[s]
                            else:
                                r2 = l * R2_IN[s] + i * 32 + (16 * b + R2_BASE[s])
                            pe.wait_ge(r2_in[s], r2)
                            wv = ring2[s].rearrange("p (k n) -> p k n", k=4)
                            for k in range(4):
                                for half in range(2):
                                    ins = mm(ps[CAP * half:CAP * half + CAP, bank, :], lhs(k), wv[:, k, 512 * half:512 * half + 512],
                                             start=(first and k == 0), stop=(last and k == 3))
                            return ins

                        for m, (bank, name) in enumerate(((2 * b, "g_ps"), (2 * b + 1, "u_ps"))):
                            for q in range(2):
                                s = 6 + q if (m, b) == (0, 1) else 2 * m + q
                                ins = halves(bank, lambda k: xsT[b][:, 4 * q + k, :], s, q == 0, q == 1)
                                if q == 1:
                                    ins.then_inc(sm[name], 1)
                                elif s < 6:
                                    ins.then_inc(r2_used[s], 1)
                        pe.wait_ge(sm["hid_done"], n + 1)
                        for c in range(4):
                            ins = tr(ps[:, 4, P * c:P * c + P], hid[b][:, P * c:P * c + P], ident)
                        ins.then_inc(sm["ht_ps"], 1)
                        pe.wait_ge(sm["ht_copied"], n + 1)
                        for q in range(2):
                            ins = halves(6 + b, lambda k: hT2[b][:, k, CAP * q:CAP * q + CAP], 4 + q, q == 0, q == 1)
                            ins.then_inc(r2_used[4] if q == 0 else sm["y2_ps"], 1)

        @block.gpsimd
        def _(pool):
            G = nc.gpsimd
            waits = Settle(pool, sm["settled"])
            chain = Chain(waits, sm["pool_step"])
            mul, add = ALU.mult, ALU.add
            cond = small[:, 13, :]
            waits.wait_ge(sm["cond"], 1)

            def mod_blocks(l, j0, pairs, done):
                with pool.Fori(0, pairs) as i:
                    n0 = chain.enter(i, 28)
                    for b in range(2):
                        n = 6 * l + j0 + b
                        col = i * (2 * D) + (j0 + b) * D

                        def load(k):
                            pool.dma_start(mod_in[k % 2], a["w_mod"][l][P * k:P * k + P, bass.ds(col, D)]) \
                                .then_inc(mod_in_s[k % 2], 16)

                        load(0)
                        load(1)
                        waits.wait_ge(sm["mod_ps"], i * 2 + (n - 1))
                        for k in range(KC):
                            waits.wait_ge(mod_in_s[k % 2], i * 128 + (64 * (done + b) + 16 * (k // 2 + 1)))
                            if k == 0:
                                chain(G.tensor_scalar(mod_acc[b], mod_in[0], cond[:, 0:1], None, mul))
                            else:
                                chain(G.tensor_scalar(mod_t, mod_in[k % 2], cond[:, k:k + 1], None, mul))
                            if k + 2 < KC:
                                load(k + 2)
                            if k > 0:
                                ins = G.tensor_tensor(mod_acc[b], mod_acc[b], mod_t, add)
                                if k < KC - 1:
                                    chain(ins)
                                else:
                                    ins.then_inc(sm["mod_sum"], 1)
                    chain.leave(n0, pairs)

            mod_blocks(0, 2, 2, 0)
            mod_blocks(1, 0, 3, 4)

            with pool.Fori(0, DEPTH) as l:
                waits.wait_ge(sm["qk_normed"], l + 1)
                waits.wait_ge(sm["conv_out"], l + 1)
                for kind in range(2):
                    with pool.Fori(0, 3) as p:
                        waits.wait_ge(sm["stage_free"], l * 6 + p + (3 * kind + 1))
                        if kind == 0:
                            for i, dst in enumerate((stage_qa, stage_ka)):
                                G.tensor_copy(dst, qk[:, :, bass.ds(p * P + A_W * i, P)]).then_inc(sm["staged"], 1)
                            for i in range(2):
                                waits.wait_ge(bias_in[i], l * 96 + p * 32 + 32)
                                b = bias[i][:, :, 0:GRID]
                                mask = const[:, C_MASK:C_MASK + GRID].unsqueeze(1).to_broadcast([P, 14, GRID])
                                G.tensor_tensor(b, b, mask, add).then_inc(sm["bias_ready"], 1)
                        else:
                            for dst, x in ((stage_q, qb), (stage_k, kb)):
                                G.tensor_copy(dst, x[:, :, bass.ds(p * 2, 2), :]).then_inc(sm["staged"], 1)

                waits.wait_ge(sm["idx_cols"], l + 1)
                waits.wait_ge(sm["xn_saved"], l * 16 + 16)
                waits.wait_ge(sm["acc_saved"], l * 16 + 16)

                def gather(e, b, k):
                    G.tensor_copy(get_c[b][:, :], get_i[0:CAP, e:e + 1] if isinstance(e, int) else get_i[0:CAP, bass.ds(e, 1)]) \
                        .then_inc(sm["get_col"], 1)
                    waits.wait_ge(sm["get_col"], k)
                    G.indirect_dma_start(out=xg[b][0:CAP], out_offset=None, in_=xn_dram,
                                         in_offset=bass.IndirectOffsetOnAxis(ap=get_c[b][:, 0:1], axis=0)).then_inc(got[b], 16)

                def scatter(e, b):
                    n = l * 16 + e
                    G.tensor_copy(put_c[b][:, :], put_i[:, e:e + 1] if isinstance(e, int) else put_i[:, bass.ds(e, 1)]) \
                        .then_inc(sm["put_col"], 1)
                    waits.wait_ge(sm["put_col"], n + 1)
                    waits.wait_ge(sm["ye_done"], n + 1)
                    G.indirect_dma_start(out=out_rows, out_offset=bass.IndirectOffsetOnAxis(ap=put_c[b][:, 0:1], axis=0),
                                         in_=ye[b], in_offset=None, compute_op=add).then_inc(put[b], 16)

                def scattered(e, b):
                    waits.wait_ge(put[b], l * 128 + 16 + (e - b) * 8)
                    pool.sem_inc(sm["put_free"], 1)

                gather(0, 0, l * 16 + 1)
                gather(1, 1, l * 16 + 2)
                with pool.Fori(0, EXPERTS // 2 - 1) as i:
                    for b in range(2):
                        scatter(i * 2 + b, b)
                        waits.wait_ge(sm["xst_ps"], l * 16 + i * 2 + (b + 1))
                        gather(i * 2 + (b + 2), b, l * 16 + i * 2 + (b + 3))
                        scattered(i * 2 + b, b)
                for b in range(2):
                    scatter(EXPERTS - 2 + b, b)
                    scattered(EXPERTS - 2 + b, b)


def constants():
    import numpy as np
    c = np.zeros((P, C_N), np.float32)
    p = np.arange(P)
    c[p, C_ID + p] = 1
    c[p, C_FLIP + (p // GRID) * GRID + GRID - 1 - p % GRID] = 1
    col = GRID - 1 - p % GRID
    first = np.clip(col - 8, 0, GRID - 16)
    j = np.arange(GRID)
    c[:, C_MASK:C_MASK + GRID] = np.where((j >= first[:, None]) & (j < first[:, None] + 16), 0, -1e30)
    half = ROPE // 2
    inv = np.float32(10000.0) ** (-np.arange(half, dtype=np.float32) / np.float32(half))
    pos = (np.arange(TC)[None, :] * P + p[:, None]).astype(np.float32)
    ang = (pos[:, :, None] * inv[None, None, :]).astype(np.float32)
    c[:, C_COS:C_COS + 64] = np.cos(ang).reshape(P, 64)
    c[:, C_SIN:C_SIN + 64] = np.sin(ang).reshape(P, 64)
    for g, w in enumerate(WINDOWS):
        c[:, C_INV + 16 * g:C_INV + 16 * g + 16] = 1.0 / np.minimum(np.arange(1, 17), w)
    return c


_INS = ["x", "c", "w_mod", "b_mod", "norm_mix_g", "norm_ffn_g", "lru_w_y", "lru_b_y", "lru_w_in", "lru_b_in",
        "lru_conv_w", "lru_conv_b", "lru_w_a", "lru_b_a", "lru_w_x", "lru_b_x", "lru_lambda", "lru_w_out",
        "lru_b_out", "pool_w", "pool_scale", "ffn_w1", "ffn_w2", "final_norm_g", "norm_mix_2", "w_in_2",
        "q_norm_a_2", "k_norm_a_2", "rpb_2", "cq_norm_2", "w_uq_2", "ckv_norm_2", "w_ukv_2", "q_norm_b_2",
        "k_norm_b_2", "conv_w_2", "out_norm_2", "w_out_2", "norm_ffn_2", "w_router_2", "b_router_2",
        "w_gate_2", "w_up_2", "w_down_2"]


def kernel(**inputs):
    import numpy as np
    import concourse.bacc as bacc
    from concourse.bass_utils import run_bass_kernel_spmd as run

    nc = bacc.Bacc("TRN2", target_bir_lowering=False, num_devices=1)
    arrays, aps = {}, {}
    for name in _INS:
        arr = np.ascontiguousarray(inputs[name])
        arrays[f"in_{name}"] = arr
        aps[name] = nc.dram_tensor(f"in_{name}", arr.shape, mybir.dt.from_np(arr.dtype), kind="ExternalInput").ap()
    arrays["consts"] = constants()
    aps["consts"] = nc.dram_tensor("consts", (P, C_N), F32, kind="ExternalInput").ap()
    out = nc.dram_tensor("out", (1, S, D), F32, kind="ExternalOutput").ap()
    program(nc, aps, out)
    r = run(nc, [arrays], core_ids=[0])
    return r.results[0]["out"]
```
